# Optimizing a Trainium2 kernel written in Bass

```python
import jax, jax.numpy as jnp
from jax import lax
import numpy as np
import jax
import jax.numpy as jnp

D_MODEL = 1024
BATCH = 1
SEQ = 512
DEPTH = 2

N_A_LAYERS = DEPTH // 2
N_B_LAYERS = DEPTH - N_A_LAYERS
HEAD_DIM = 64
MIX_WIDTH = D_MODEL
MEM_HEADS = 4
MEM_WIDTH = MEM_HEADS * HEAD_DIM
N_MEM = 256
LRU_WIDTH = MIX_WIDTH - MEM_WIDTH
LRU_BLOCKS = 6
LRU_BLOCK = LRU_WIDTH // LRU_BLOCKS
CONV_WIDTH = 4
LRU_C = 8.0
SWA_Q_HEADS = (MIX_WIDTH - MEM_WIDTH) // HEAD_DIM
SWA_KV_HEADS = 4
SWA_GROUP = SWA_Q_HEADS // SWA_KV_HEADS
KV_WIDTH = SWA_KV_HEADS * HEAD_DIM
WINDOW = 128
BLOCK = 128
ROPE_DIM = HEAD_DIM // 4
ROPE_THETA = 500000.0
D_FF = -(-8 * D_MODEL // (3 * 256)) * 256
A_IN_WIDTH = 2 * LRU_WIDTH + MEM_WIDTH
B_IN_WIDTH = SWA_Q_HEADS * HEAD_DIM + MEM_WIDTH
EPS = 1e-6
NEG_INF = -1e30


def rms_norm(x, g):
    xf = x.astype(jnp.float32)
    y = xf * lax.rsqrt(jnp.mean(xf * xf, axis=-1, keepdims=True) + EPS)
    return (y * g.astype(jnp.float32)).astype(x.dtype)

def rope_tables(seq):
    inv_freq = 1.0 / (ROPE_THETA ** (jnp.arange(0, ROPE_DIM, 2, dtype=jnp.float32) / ROPE_DIM))
    ang = jnp.arange(seq, dtype=jnp.float32)[:, None] * inv_freq[None, :]
    return jnp.cos(ang), jnp.sin(ang)

def apply_partial_rope(x, cos, sin):
    half = ROPE_DIM // 2
    xr = x[..., :ROPE_DIM].astype(jnp.float32)
    x1, x2 = xr[..., :half], xr[..., half:]
    c = cos[None, :, None, :]
    s = sin[None, :, None, :]
    rot = jnp.concatenate([x1 * c - x2 * s, x2 * c + x1 * s], axis=-1).astype(x.dtype)
    return jnp.concatenate([rot, x[..., ROPE_DIM:]], axis=-1)

def causal_depthwise_conv(x, w, b):
    c = x.shape[-1]
    y = lax.conv_general_dilated(
        x, w[:, None, :].astype(x.dtype), window_strides=(1,),
        padding=[(CONV_WIDTH - 1, 0)], dimension_numbers=("NWC", "WIO", "NWC"),
        feature_group_count=c)
    return y + b

def _linear_recurrence_combine(left, right):
    a1, b1 = left
    a2, b2 = right
    return a1 * a2, a2 * b1 + b2

def rg_lru(x, w_r, b_r, w_i, b_i, lam):
    bsz, seq, width = x.shape
    xb = x.reshape(bsz, seq, LRU_BLOCKS, LRU_BLOCK)
    r = jax.nn.sigmoid(jnp.einsum("bshi,hij->bshj", xb, w_r)
                       + b_r.reshape(LRU_BLOCKS, LRU_BLOCK)).reshape(bsz, seq, width)
    i = jax.nn.sigmoid(jnp.einsum("bshi,hij->bshj", xb, w_i)
                       + b_i.reshape(LRU_BLOCKS, LRU_BLOCK)).reshape(bsz, seq, width)
    log_a = LRU_C * r.astype(jnp.float32) * jax.nn.log_sigmoid(lam.astype(jnp.float32))
    a = jnp.exp(log_a)
    mult = jnp.sqrt(jnp.maximum(1.0 - jnp.exp(2.0 * log_a), 0.0))
    first = (jnp.arange(seq) == 0)[None, :, None]
    mult = jnp.where(first, 1.0, mult)
    u = mult * (i * x).astype(jnp.float32)
    _, h = lax.associative_scan(_linear_recurrence_combine, (a, u), axis=1)
    return h.astype(x.dtype)

def sliding_window_attention_with_sinks(q, k, v, sinks):
    bsz, seq = q.shape[0], q.shape[1]
    nb = seq // BLOCK
    qb = q.reshape(bsz, nb, BLOCK, SWA_KV_HEADS, SWA_GROUP, HEAD_DIM)

    def band(t):
        cur = t.reshape(bsz, nb, BLOCK, SWA_KV_HEADS, HEAD_DIM)
        prev = jnp.concatenate([jnp.zeros_like(cur[:, :1]), cur[:, :-1]], axis=1)
        return jnp.concatenate([prev, cur], axis=2)

    kb, vb = band(k), band(v)
    scores = jnp.einsum("bnqkgd,bnckd->bnkgqc", qb, kb).astype(jnp.float32) * (HEAD_DIM ** -0.5)
    qi = jnp.arange(BLOCK)[:, None] + BLOCK
    ci = jnp.arange(2 * BLOCK)[None, :]
    rel = qi - ci
    in_window = (rel >= 0) & (rel < WINDOW)
    has_prev = (jnp.arange(nb) > 0)[:, None, None] | (ci >= BLOCK)[None]
    mask = in_window[None] & has_prev
    scores = jnp.where(mask[None, :, None, None], scores, NEG_INF)
    sink = sinks.astype(jnp.float32).reshape(1, 1, SWA_KV_HEADS, SWA_GROUP, 1, 1)
    m = jnp.maximum(jnp.max(scores, axis=-1, keepdims=True), sink)
    e = jnp.exp(scores - m)
    probs = e / (jnp.sum(e, axis=-1, keepdims=True) + jnp.exp(sink - m))
    out = jnp.einsum("bnkgqc,bnckd->bnqkgd", probs.astype(v.dtype), vb)
    return out.reshape(bsz, seq, SWA_Q_HEADS * HEAD_DIM)

def memory_attention(q, mk, mv):
    bsz, seq = q.shape[0], q.shape[1]
    s = jnp.einsum("bshd,bmhd->bhsm", q, mk).astype(jnp.float32) * (HEAD_DIM ** -0.5)
    p = jax.nn.softmax(s, axis=-1).astype(mv.dtype)
    o = jnp.einsum("bhsm,bmhd->bshd", p, mv)
    return o.reshape(bsz, seq, MEM_WIDTH)

def swiglu_ffn(x, w_in, w_out):
    gu = x @ w_in
    g, u = gu[..., :D_FF], gu[..., D_FF:]
    return (jax.nn.silu(g) * u) @ w_out

def first_inputs(seed: int = 0) -> dict:
    key = jax.random.key(seed)
    ks = jax.random.split(key, 24)

    def nrm(k, shape, scale):
        return jax.random.normal(k, shape, dtype=jnp.float32) * scale

    def gain(k, shape):
        return 1.0 + 0.05 * jax.random.normal(k, shape, dtype=jnp.float32)

    u = jax.random.uniform(ks[14], (N_A_LAYERS, LRU_WIDTH), dtype=jnp.float32,
                           minval=0.81, maxval=0.998)
    a0 = jnp.sqrt(u)
    lru_lambda = jnp.log(a0) - jnp.log1p(-a0)
    return {
        "x": nrm(ks[0], (BATCH, SEQ, D_MODEL), 1.0),
        "mem": nrm(ks[1], (BATCH, N_MEM, D_MODEL), 1.0),
        "norm_mix_pre": gain(ks[2], (DEPTH, D_MODEL)),
        "norm_mix_post": gain(ks[3], (DEPTH, D_MODEL)),
        "norm_ffn_pre": gain(ks[4], (DEPTH, D_MODEL)),
        "norm_ffn_post": gain(ks[5], (DEPTH, D_MODEL)),
        "mem_norm": gain(ks[6], (D_MODEL,)),
        "w_mem_kv": nrm(ks[7], (DEPTH, D_MODEL, 2 * MEM_WIDTH), D_MODEL ** -0.5),
        "w_in_a": nrm(ks[8], (N_A_LAYERS, D_MODEL, A_IN_WIDTH), D_MODEL ** -0.5),
        "conv_w": nrm(ks[9], (N_A_LAYERS, CONV_WIDTH, LRU_WIDTH), CONV_WIDTH ** -0.5),
        "conv_b": nrm(ks[10], (N_A_LAYERS, LRU_WIDTH), 0.02),
        "w_gate_r": nrm(ks[11], (N_A_LAYERS, LRU_BLOCKS, LRU_BLOCK, LRU_BLOCK), LRU_BLOCK ** -0.5),
        "b_gate_r": nrm(ks[12], (N_A_LAYERS, LRU_WIDTH), 0.02),
        "w_gate_i": nrm(ks[13], (N_A_LAYERS, LRU_BLOCKS, LRU_BLOCK, LRU_BLOCK), LRU_BLOCK ** -0.5),
        "b_gate_i": nrm(ks[15], (N_A_LAYERS, LRU_WIDTH), 0.02),
        "lru_lambda": lru_lambda,
        "norm_kv": gain(ks[16], (D_MODEL,)),
        "w_kv_shared": nrm(ks[17], (D_MODEL, 2 * KV_WIDTH), D_MODEL ** -0.5),
        "w_in_b": nrm(ks[18], (N_B_LAYERS, D_MODEL, B_IN_WIDTH), D_MODEL ** -0.5),
        "sinks": nrm(ks[19], (N_B_LAYERS, SWA_Q_HEADS), 1.0),
        "w_out": nrm(ks[20], (DEPTH, MIX_WIDTH, D_MODEL), MIX_WIDTH ** -0.5),
        "w_ffn_in": nrm(ks[21], (DEPTH, D_MODEL, 2 * D_FF), D_MODEL ** -0.5),
        "w_ffn_out": nrm(ks[22], (DEPTH, D_FF, D_MODEL), D_FF ** -0.5),
    }

def first_block(x, mem, norm_mix_pre, norm_mix_post, norm_ffn_pre, norm_ffn_post, mem_norm,
              w_mem_kv, w_in_a, conv_w, conv_b, w_gate_r, b_gate_r, w_gate_i, b_gate_i,
              lru_lambda, norm_kv, w_kv_shared, w_in_b, sinks, w_out, w_ffn_in, w_ffn_out):
    bsz, seq = x.shape[0], x.shape[1]
    n_mem = mem.shape[1]
    cos, sin = rope_tables(seq)
    mem_n = rms_norm(mem, mem_norm)
    h = x
    shared_k = None
    shared_v = None
    for l in range(DEPTH):
        hn = rms_norm(h, norm_mix_pre[l])
        mkv = mem_n @ w_mem_kv[l]
        mk = mkv[..., :MEM_WIDTH].reshape(bsz, n_mem, MEM_HEADS, HEAD_DIM)
        mv = mkv[..., MEM_WIDTH:].reshape(bsz, n_mem, MEM_HEADS, HEAD_DIM)
        if l < N_A_LAYERS:
            a = l
            proj = hn @ w_in_a[a]
            xr = proj[..., :LRU_WIDTH]
            gate = proj[..., LRU_WIDTH:2 * LRU_WIDTH]
            mq = proj[..., 2 * LRU_WIDTH:].reshape(bsz, seq, MEM_HEADS, HEAD_DIM)
            xr = causal_depthwise_conv(xr, conv_w[a], conv_b[a])
            y = rg_lru(xr, w_gate_r[a], b_gate_r[a], w_gate_i[a], b_gate_i[a], lru_lambda[a])
            y = y * jax.nn.gelu(gate)
        else:
            b = l - N_A_LAYERS
            proj = hn @ w_in_b[b]
            q = proj[..., :SWA_Q_HEADS * HEAD_DIM].reshape(bsz, seq, SWA_Q_HEADS, HEAD_DIM)
            mq = proj[..., SWA_Q_HEADS * HEAD_DIM:].reshape(bsz, seq, MEM_HEADS, HEAD_DIM)
            q = apply_partial_rope(q, cos, sin)
            y = sliding_window_attention_with_sinks(q, shared_k, shared_v, sinks[b])
        m_out = memory_attention(mq, mk, mv)
        mixed = jnp.concatenate([y, m_out], axis=-1) @ w_out[l]
        h = h + rms_norm(mixed, norm_mix_post[l])
        f = swiglu_ffn(rms_norm(h, norm_ffn_pre[l]), w_ffn_in[l], w_ffn_out[l])
        h = h + rms_norm(f, norm_ffn_post[l])
        if l == N_A_LAYERS - 1:
            kv = rms_norm(h, norm_kv) @ w_kv_shared
            shared_k = apply_partial_rope(
                kv[..., :KV_WIDTH].reshape(bsz, seq, SWA_KV_HEADS, HEAD_DIM), cos, sin)
            shared_v = kv[..., KV_WIDTH:].reshape(bsz, seq, SWA_KV_HEADS, HEAD_DIM)
    return h


DEPTH_2 = 1

GRID_W = 64
CTX_LEN = 256
D_MIX = D_MODEL
D_MLSTM = D_MIX // 2
MLSTM_HEADS = 4
MLSTM_DH = D_MLSTM // MLSTM_HEADS
QKV_BLOCK = 4
N_QKV_BLOCKS = D_MLSTM // QKV_BLOCK
CONV_K = 3
CHUNK = 128
D_FOURIER = D_MIX - D_MLSTM
FOURIER_GROUPS = 4
FOURIER_CG = D_FOURIER // FOURIER_GROUPS
D_IN_PROJ = 2 * D_MLSTM + D_FOURIER
N_EXPERT_GROUPS = 4
EXPERTS_PER_GROUP = 4
N_EXPERTS = N_EXPERT_GROUPS * EXPERTS_PER_GROUP
TOP_K = 2
D_EXPERT = D_MODEL // 2
N_MOD = 6
POS_BASE = 10000.0
F32 = jnp.float32


def rmsnorm(x, g):
    x32 = x.astype(F32)
    y = x32 * lax.rsqrt(jnp.mean(x32 * x32, axis=-1, keepdims=True) + EPS)
    return (y * g.astype(F32)).astype(x.dtype)

def modulate(h, shift, scale):
    return h * (1 + scale) + shift

def sincos_2d(rows, cols):
    quarter = D_MODEL // 4
    freq = 1.0 / (POS_BASE ** (jnp.arange(quarter, dtype=F32) / quarter))
    r = jnp.arange(rows, dtype=F32)[:, None] * freq
    cl = jnp.arange(cols, dtype=F32)[:, None] * freq
    er = jnp.concatenate([jnp.sin(r), jnp.cos(r)], axis=-1)
    ec = jnp.concatenate([jnp.sin(cl), jnp.cos(cl)], axis=-1)
    half = D_MODEL // 2
    emb = jnp.concatenate([jnp.broadcast_to(er[:, None, :], (rows, cols, half)),
                           jnp.broadcast_to(ec[None, :, :], (rows, cols, half))], axis=-1)
    return emb.reshape(rows * cols, D_MODEL)

def short_conv(x, w, b):
    y = lax.conv_general_dilated(x, w[:, None, :], window_strides=(1,), padding='SAME',
                                 dimension_numbers=('NWC', 'WIO', 'NWC'),
                                 feature_group_count=x.shape[-1])
    return y + b

def headwise(x, w):
    y = jnp.einsum('btni,nio->btno', x.reshape(x.shape[:-1] + (N_QKV_BLOCKS, QKV_BLOCK)), w)
    return y.reshape(x.shape)

def to_heads(t):
    B, T, _ = t.shape
    return t.astype(F32).reshape(B, T, MLSTM_HEADS, MLSTM_DH).transpose(0, 2, 1, 3)

def flip_seq(t):
    return jnp.flip(t, axis=2)

def mixer_features(h, lp):
    proj = h @ lp['w_in']
    x_m = proj[..., :D_MLSTM]
    z = proj[..., D_MLSTM:2 * D_MLSTM]
    u = proj[..., 2 * D_MLSTM:]
    act = jax.nn.silu(short_conv(x_m, lp['conv_w'], lp['conv_b']))
    q = headwise(act, lp['w_q'])
    k = headwise(act, lp['w_k'])
    v = headwise(x_m, lp['w_v'])
    qkv = jnp.concatenate([q, k, v], axis=-1)

    def gates(w, b):
        g = (qkv @ w + b).astype(F32).transpose(0, 2, 1)
        return g[:, :MLSTM_HEADS], jax.nn.log_sigmoid(g[:, MLSTM_HEADS:])

    heads = (to_heads(q) * (MLSTM_DH ** -0.5), to_heads(k), to_heads(v))
    return heads, gates(lp['w_if_fwd'], lp['b_if_fwd']), gates(lp['w_if_bwd'], lp['b_if_bwd']), act, z, u

def mlstm_scan(k, v, ig, lf, state):
    B, H, T, DH = k.shape
    nc = T // CHUNK
    kc = k.reshape(B, H, nc, CHUNK, DH)
    vc = v.reshape(B, H, nc, CHUNK, DH)
    b = jnp.cumsum(lf.reshape(B, H, nc, CHUNK), axis=-1)
    btot = b[..., -1]
    a = btot[..., None] - b + ig.reshape(B, H, nc, CHUNK)
    amax = jnp.max(a, axis=-1)

    def step(carry, xs):
        C, n, m = carry
        k_, v_, a_, amax_, bt_ = xs
        m_new = jnp.maximum(bt_ + m, amax_)
        decay = jnp.exp(bt_ + m - m_new)
        kw = k_ * jnp.exp(a_ - m_new[..., None])[..., None]
        C_new = decay[..., None, None] * C + jnp.einsum('bhlk,bhlv->bhkv', kw, v_)
        n_new = decay[..., None] * n + jnp.sum(kw, axis=2)
        return (C_new, n_new, m_new), (C, n, m)

    xs = tuple(jnp.moveaxis(t, 2, 0) for t in (kc, vc, a, amax, btot))
    final, starts = lax.scan(step, state, xs)
    starts = tuple(jnp.moveaxis(s, 0, 2) for s in starts)
    return starts, final

def mlstm_out(q, k, v, ig, lf, starts):
    C0, n0, m0 = starts
    B, H, T, DH = q.shape
    nc = T // CHUNK
    qc = q.reshape(B, H, nc, CHUNK, DH)
    kc = k.reshape(B, H, nc, CHUNK, DH)
    vc = v.reshape(B, H, nc, CHUNK, DH)
    igc = ig.reshape(B, H, nc, CHUNK)
    b = jnp.cumsum(lf.reshape(B, H, nc, CHUNK), axis=-1)
    tri = jnp.tril(jnp.ones((CHUNK, CHUNK), dtype=bool))
    logd = jnp.where(tri, b[..., :, None] - b[..., None, :] + igc[..., None, :], -jnp.inf)
    m_inter = b + m0[..., None]
    m_t = jnp.maximum(m_inter, jnp.max(logd, axis=-1))
    w_inter = jnp.exp(m_inter - m_t)
    s = jnp.einsum('bhctd,bhcsd->bhcts', qc, kc) * jnp.exp(logd - m_t[..., None])
    num = jnp.einsum('bhcts,bhcsd->bhctd', s, vc) + w_inter[..., None] * jnp.einsum('bhctk,bhckv->bhctv', qc, C0)
    nq = jnp.sum(s, axis=-1) + w_inter * jnp.einsum('bhctk,bhck->bhct', qc, n0)
    h = num / jnp.maximum(jnp.abs(nq), jnp.exp(-m_t))[..., None]
    return h.reshape(B, H, T, DH)

def mlstm_direction(ctx_in, lat_in, with_ctx):
    qc, kc, vc, igc, lfc = ctx_in
    ql, kl, vl, igl, lfl = lat_in
    B = kl.shape[0]
    zero = (jnp.zeros((B, MLSTM_HEADS, MLSTM_DH, MLSTM_DH), F32),
            jnp.zeros((B, MLSTM_HEADS, MLSTM_DH), F32),
            jnp.zeros((B, MLSTM_HEADS), F32))
    ctx_starts, ctx_final = mlstm_scan(kc, vc, igc, lfc, zero)
    lat_starts, _ = mlstm_scan(kl, vl, igl, lfl, ctx_final)
    h_lat = mlstm_out(ql, kl, vl, igl, lfl, lat_starts)
    h_ctx = mlstm_out(qc, kc, vc, igc, lfc, ctx_starts) if with_ctx else None
    return h_lat, h_ctx

def mlstm_readout(hf, hb, act, z, norm_w, skip):
    h = hf + hb
    mu = jnp.mean(h, axis=-1, keepdims=True)
    var = jnp.mean(jnp.square(h - mu), axis=-1, keepdims=True)
    hn = (h - mu) * lax.rsqrt(var + EPS)
    B, H, T, DH = hn.shape
    hn = hn.transpose(0, 2, 1, 3).reshape(B, T, D_MLSTM) * norm_w.astype(F32)
    out = (hn + skip.astype(F32) * act.astype(F32)) * jax.nn.silu(z.astype(F32))
    return out.astype(z.dtype)

def fourier_mix(u, w_fourier):
    B, T, _ = u.shape
    ug = u.astype(F32).reshape(B, T, FOURIER_GROUPS, FOURIER_CG)
    f = jnp.fft.fft2(ug, axes=(1, 3), norm='ortho').real
    y = jnp.einsum('btgc,gcd->btgd', f, w_fourier.astype(F32))
    return y.reshape(B, T, D_FOURIER).astype(u.dtype)

def token_mix(h, hc, lp, with_ctx):
    qkv_l, gf_l, gb_l, act_l, z_l, u_l = mixer_features(h, lp)
    qkv_c, gf_c, gb_c, act_c, z_c, u_c = mixer_features(hc, lp)
    hf_l, hf_c = mlstm_direction(qkv_c + gf_c, qkv_l + gf_l, with_ctx)
    hb_l, hb_c = mlstm_direction(tuple(flip_seq(t) for t in qkv_c + gb_c),
                                 tuple(flip_seq(t) for t in qkv_l + gb_l), with_ctx)

    def merge(hf, hb, act, z, u):
        m = mlstm_readout(hf, flip_seq(hb), act, z, lp['mlstm_norm_w'], lp['mlstm_skip'])
        f = fourier_mix(u, lp['w_fourier'])
        return jnp.concatenate([m, f], axis=-1) @ lp['w_out']

    y_l = merge(hf_l, hb_l, act_l, z_l, u_l)
    y_c = merge(hf_c, hb_c, act_c, z_c, u_c) if with_ctx else None
    return y_l, y_c

def hier_moe(h, lp):
    B, T, _ = h.shape
    g_logits = (h @ lp['w_router_group'] + lp['b_router_group']).astype(F32)
    p_group = jax.nn.softmax(g_logits, axis=-1)
    g_sel = jnp.argmax(g_logits, axis=-1)
    p_sel = jnp.take_along_axis(p_group, g_sel[..., None], axis=-1)
    e_logits = (h @ lp['w_router_expert'] + lp['b_router_expert']).astype(F32)
    e_logits = e_logits.reshape(B, T, N_EXPERT_GROUPS, EXPERTS_PER_GROUP)
    e_sel = jnp.take_along_axis(e_logits, g_sel[..., None, None], axis=2)[..., 0, :]
    top_v, top_i = lax.top_k(e_sel, TOP_K)
    w_top = jax.nn.softmax(top_v, axis=-1) * p_sel
    expert_id = g_sel[..., None] * EXPERTS_PER_GROUP + top_i
    combine = jnp.sum(jax.nn.one_hot(expert_id, N_EXPERTS, dtype=F32) * w_top[..., None], axis=-2)
    combine = combine.astype(h.dtype)
    y = jnp.zeros_like(h)
    for e in range(N_EXPERTS):
        a = jax.nn.silu(h @ lp['w_gate'][e]) * (h @ lp['w_up'][e])
        y = y + combine[..., e, None] * (a @ lp['w_down'][e])
    return y

def second_inputs(seed: int = 0) -> dict:
    key = jax.random.key(seed)
    ks = jax.random.split(key, 40)
    L = DEPTH_2
    H = MLSTM_HEADS

    def nrm(k, shape, s):
        return jax.random.normal(k, shape, F32) * s

    def b_if(k1, k2):
        return jnp.concatenate([nrm(k1, (L, H), 0.1),
                                jnp.linspace(3.0, 6.0, H, dtype=F32)[None, :] + nrm(k2, (L, H), 0.1)], axis=-1)

    return {
        'x': nrm(ks[0], (BATCH, SEQ, D_MODEL), 1.0),
        'c': nrm(ks[1], (BATCH, D_MODEL), 1.0),
        'ctx': nrm(ks[2], (BATCH, CTX_LEN, D_MODEL), 1.0),
        'c_ctx': nrm(ks[3], (D_MODEL,), 1.0),
        'w_ada': nrm(ks[4], (L, D_MODEL, N_MOD * D_MODEL), 0.5 * D_MODEL ** -0.5),
        'b_ada': nrm(ks[5], (L, N_MOD * D_MODEL), 0.01),
        'g_pre_mix': 1.0 + nrm(ks[6], (L, D_MODEL), 0.05),
        'g_post_mix': 1.0 + nrm(ks[7], (L, D_MODEL), 0.05),
        'g_pre_ffn': 1.0 + nrm(ks[8], (L, D_MODEL), 0.05),
        'g_post_ffn': 1.0 + nrm(ks[9], (L, D_MODEL), 0.05),
        'w_in': nrm(ks[10], (L, D_MODEL, D_IN_PROJ), D_MODEL ** -0.5),
        'conv_w': nrm(ks[11], (L, CONV_K, D_MLSTM), CONV_K ** -0.5),
        'conv_b': nrm(ks[12], (L, D_MLSTM), 0.01),
        'w_q': nrm(ks[13], (L, N_QKV_BLOCKS, QKV_BLOCK, QKV_BLOCK), QKV_BLOCK ** -0.5),
        'w_k': nrm(ks[14], (L, N_QKV_BLOCKS, QKV_BLOCK, QKV_BLOCK), QKV_BLOCK ** -0.5),
        'w_v': nrm(ks[15], (L, N_QKV_BLOCKS, QKV_BLOCK, QKV_BLOCK), QKV_BLOCK ** -0.5),
        'w_if_fwd': nrm(ks[16], (L, 3 * D_MLSTM, 2 * H), 0.02),
        'b_if_fwd': b_if(ks[17], ks[18]),
        'w_if_bwd': nrm(ks[19], (L, 3 * D_MLSTM, 2 * H), 0.02),
        'b_if_bwd': b_if(ks[20], ks[21]),
        'mlstm_norm_w': 1.0 + nrm(ks[22], (L, D_MLSTM), 0.05),
        'mlstm_skip': 1.0 + nrm(ks[23], (L, D_MLSTM), 0.05),
        'w_fourier': nrm(ks[24], (L, FOURIER_GROUPS, FOURIER_CG, FOURIER_CG), FOURIER_CG ** -0.5),
        'w_out': nrm(ks[25], (L, D_MIX, D_MODEL), D_MIX ** -0.5),
        'w_router_group': nrm(ks[26], (L, D_MODEL, N_EXPERT_GROUPS), D_MODEL ** -0.5),
        'b_router_group': nrm(ks[27], (L, N_EXPERT_GROUPS), 0.01),
        'w_router_expert': nrm(ks[28], (L, D_MODEL, N_EXPERTS), D_MODEL ** -0.5),
        'b_router_expert': nrm(ks[29], (L, N_EXPERTS), 0.01),
        'w_gate': nrm(ks[30], (L, N_EXPERTS, D_MODEL, D_EXPERT), D_MODEL ** -0.5),
        'w_up': nrm(ks[31], (L, N_EXPERTS, D_MODEL, D_EXPERT), D_MODEL ** -0.5),
        'w_down': nrm(ks[32], (L, N_EXPERTS, D_EXPERT, D_MODEL), D_EXPERT ** -0.5),
    }

def second_block(x, c, ctx, c_ctx, w_ada, b_ada, g_pre_mix, g_post_mix, g_pre_ffn, g_post_ffn,
              w_in, conv_w, conv_b, w_q, w_k, w_v, w_if_fwd, b_if_fwd, w_if_bwd, b_if_bwd,
              mlstm_norm_w, mlstm_skip, w_fourier, w_out, w_router_group, b_router_group,
              w_router_expert, b_router_expert, w_gate, w_up, w_down):
    T = x.shape[1]
    rows = T // GRID_W
    x = x + sincos_2d(rows, GRID_W).astype(x.dtype)[None]
    xc = ctx
    for l in range(DEPTH_2):
        with_ctx = l + 1 < DEPTH_2
        lp = {
            'w_in': w_in[l], 'conv_w': conv_w[l], 'conv_b': conv_b[l],
            'w_q': w_q[l], 'w_k': w_k[l], 'w_v': w_v[l],
            'w_if_fwd': w_if_fwd[l], 'b_if_fwd': b_if_fwd[l],
            'w_if_bwd': w_if_bwd[l], 'b_if_bwd': b_if_bwd[l],
            'mlstm_norm_w': mlstm_norm_w[l], 'mlstm_skip': mlstm_skip[l],
            'w_fourier': w_fourier[l], 'w_out': w_out[l],
            'w_router_group': w_router_group[l], 'b_router_group': b_router_group[l],
            'w_router_expert': w_router_expert[l], 'b_router_expert': b_router_expert[l],
            'w_gate': w_gate[l], 'w_up': w_up[l], 'w_down': w_down[l],
        }
        mod = [m[:, None, :] for m in jnp.split(jax.nn.silu(c) @ w_ada[l] + b_ada[l], N_MOD, axis=-1)]
        mod_c = [m[None, :] for m in jnp.split(jax.nn.silu(c_ctx) @ w_ada[l] + b_ada[l], N_MOD, axis=-1)]
        shift1, scale1, gate1, shift2, scale2, gate2 = mod
        h = modulate(rmsnorm(x, g_pre_mix[l]), shift1, scale1)
        hc = modulate(rmsnorm(xc, g_pre_mix[l]), mod_c[0], mod_c[1])
        y, yc = token_mix(h, hc, lp, with_ctx)
        x = x + gate1 * rmsnorm(y, g_post_mix[l])
        h2 = modulate(rmsnorm(x, g_pre_ffn[l]), shift2, scale2)
        x = x + gate2 * rmsnorm(hier_moe(h2, lp), g_post_ffn[l])
        if with_ctx:
            xc = xc + mod_c[2] * rmsnorm(yc, g_post_mix[l])
            hc2 = modulate(rmsnorm(xc, g_pre_ffn[l]), mod_c[3], mod_c[4])
            xc = xc + mod_c[5] * rmsnorm(hier_moe(hc2, lp), g_post_ffn[l])
    return x


def setup_inputs(seed=0):
    out = dict(first_inputs(seed))
    for name, value in second_inputs(seed + 1).items():
        if name != "x":
            out[name + "_2"] = value
    return out


def reference(
    x, mem, norm_mix_pre, norm_mix_post, norm_ffn_pre, norm_ffn_post, mem_norm, w_mem_kv,
    w_in_a, conv_w, conv_b, w_gate_r, b_gate_r, w_gate_i, b_gate_i, lru_lambda, norm_kv,
    w_kv_shared, w_in_b, sinks, w_out, w_ffn_in, w_ffn_out, c_2, ctx_2, c_ctx_2, w_ada_2,
    b_ada_2, g_pre_mix_2, g_post_mix_2, g_pre_ffn_2, g_post_ffn_2, w_in_2, conv_w_2, conv_b_2,
    w_q_2, w_k_2, w_v_2, w_if_fwd_2, b_if_fwd_2, w_if_bwd_2, b_if_bwd_2, mlstm_norm_w_2,
    mlstm_skip_2, w_fourier_2, w_out_2, w_router_group_2, b_router_group_2, w_router_expert_2,
    b_router_expert_2, w_gate_2, w_up_2, w_down_2,
):
    x = first_block(
        x, mem, norm_mix_pre, norm_mix_post, norm_ffn_pre, norm_ffn_post, mem_norm, w_mem_kv,
        w_in_a, conv_w, conv_b, w_gate_r, b_gate_r, w_gate_i, b_gate_i, lru_lambda, norm_kv,
        w_kv_shared, w_in_b, sinks, w_out, w_ffn_in, w_ffn_out,
    )
    return second_block(
        x, c_2, ctx_2, c_ctx_2, w_ada_2, b_ada_2, g_pre_mix_2, g_post_mix_2, g_pre_ffn_2,
        g_post_ffn_2, w_in_2, conv_w_2, conv_b_2, w_q_2, w_k_2, w_v_2, w_if_fwd_2, b_if_fwd_2,
        w_if_bwd_2, b_if_bwd_2, mlstm_norm_w_2, mlstm_skip_2, w_fourier_2, w_out_2,
        w_router_group_2, b_router_group_2, w_router_expert_2, b_router_expert_2, w_gate_2,
        w_up_2, w_down_2,
    )


_drawn_inputs = setup_inputs


def setup_inputs(seed=0):
    import zlib

    import numpy as np

    out = dict(_drawn_inputs(seed))
    spreads = {}
    factors = {'b_gate_r': 4.741,
     'b_gate_i': 3.34,
     'sinks': 3.397,
     'ctx_2': 2.859,
     'b_ada_2': 3.359,
     'g_pre_mix_2': 3.141,
     'g_post_mix_2': 3.848,
     'g_post_ffn_2': 8.0,
     'conv_b_2': 4.97,
     'mlstm_norm_w_2': 7.524,
     'mlstm_skip_2': 8.0,
     'b_router_group_2': 4.276,
     'b_router_expert_2': 8.0}
    for name, (base, spread) in spreads.items():
        noise = np.random.default_rng([zlib.crc32(name.encode()), seed]).standard_normal(out[name].shape)
        drawn = base * np.exp(spread * noise) if base else spread * noise
        out[name] = jnp.asarray(drawn.astype(out[name].dtype))
    for name, factor in factors.items():
        out[name] = (out[name] * factor).astype(out[name].dtype)
    return out
```

```python
from contextlib import ExitStack

import numpy as np

import concourse.bass as bass
from concourse import mybir

F32 = mybir.dt.float32
F32R = mybir.dt.float32r
U32 = mybir.dt.uint32
ALU = mybir.AluOpType
ACT = mybir.ActivationFunctionType
AX = mybir.AxisListType.X

P = 128
D = 1024
KC = D // P
T = 512
TT = T // P
TM = 256
DFF = 2816
FC = DFF // P
DH = 64
Q_HEADS, KV_HEADS, MEM_HEADS = 12, 4, 4
SCALE = DH ** -0.5
EPS = 1e-6
NEG = -1e30
LRU_C = 8.0
HALF = 1024
MH = 4
MSCALE = float(P) ** -0.5
NCH = (TM + T) // P
CTX_CH = TM // P
ROWS = 36
NE, GROUPS, PER = 16, 4, 4
DE = 512
UNITS = 12
HELD, AHEAD = 6, 4
BLOCKS = 23


class Line:

    def __init__(self, sem):
        self.sem, self.n = sem, 0

    def now(self):
        return (self, self.n)


class Queue:

    def __init__(self, eng, line):
        self.eng, self.line, self.seen = eng, line, {}

    def need(self, *tokens):
        for line, n in tokens:
            if isinstance(n, int):
                if self.seen.get(line, 0) >= n:
                    continue
                self.seen[line] = n
            self.eng.wait_ge(line.sem, n)

    def do(self, op, *args, after=(), **kw):
        self.need(*after)
        op(*args, **kw).then_inc(self.line.sem, 1)
        self.line.n += 1
        return self.line.now()


def shape_constants():
    f = np.float32
    half = DH // 4 // 2
    inv = (f(1.0) / (f(500000.0) ** (np.arange(0, DH // 4, 2, dtype=f) / f(DH // 4)))).astype(f)
    ang = (np.arange(T, dtype=f)[:, None] * inv[None, :]).astype(f).astype(np.float64)
    rope_cos, rope_sin, swap = np.ones((P, T), f), np.zeros((P, T), f), np.zeros((P, P), f)
    for p in range(P):
        r = p % DH
        if r < half:
            rope_cos[p], rope_sin[p] = np.cos(ang[:, r]), -np.sin(ang[:, r])
            swap[p + half, p] = 1
        elif r < 2 * half:
            rope_cos[p], rope_sin[p] = np.cos(ang[:, r - half]), np.sin(ang[:, r - half])
            swap[p - half, p] = 1
    q, c = np.arange(P)[:, None] + P, np.arange(2 * P)[None]
    ok = (q - c >= 0) & (q - c < P)
    band = np.where(ok, 0, NEG).astype(f)
    first = np.where(ok & (c >= P), 0, NEG).astype(f)
    window = np.stack([np.stack([first, band], 1), np.stack([band, band], 1)], 1).reshape(P, 4 * 2 * P)
    s, t = np.arange(P)[:, None], np.arange(P)[None]
    quarter = D // 4
    freq = (f(1.0) / (f(10000.0) ** (np.arange(quarter, dtype=f) / f(quarter)))).astype(f)

    def emb(n):
        a = (np.arange(n, dtype=f)[:, None] * freq).astype(f).astype(np.float64)
        e = np.concatenate([np.sin(a), np.cos(a)], -1).astype(f)
        return np.ascontiguousarray(e.T.reshape(4, P, n).transpose(1, 0, 2)).reshape(P, 4 * n)

    a128 = 2 * np.pi * ((s * t) % P) / P
    tt = np.arange(T)
    a512 = 2 * np.pi * ((tt[:, None] * tt[None]) % T) / T
    norm = 1.0 / np.sqrt(float(T * P))
    dft_t = np.concatenate([np.cos(a512), np.sin(a512)], 1) * norm
    sel = np.zeros((P, 2 * MH, P), f)
    for d in range(2):
        for h in range(MH):
            sel[32 * d + h, MH * d + h, :] = 1
    parts = {
        "ident": np.eye(P), "swap": swap, "rope_cos": rope_cos, "rope_sin": rope_sin, "window": window,
        "fwd_mask": np.where(s <= t, 0, NEG), "bwd_mask": np.where(s >= t, 0, NEG),
        "before": (s < t), "quad": (s // 4 == np.arange(32)[None]),
        "dft_c": np.concatenate([np.cos(a128), -np.sin(a128)], 1),
        "emb_row": emb(T // 64), "emb_col": emb(64), "sel": sel.reshape(P, -1),
        "iota": np.tile(np.arange(32)[None], (P, 1)), "token": s + P * np.arange(TT)[None],
    }
    where, cols, at = {}, [], 0
    for name, a in parts.items():
        a = np.asarray(a, f)
        where[name] = (at, a.shape[1])
        cols.append(a)
        at += a.shape[1]
    return np.ascontiguousarray(np.concatenate(cols, 1)), where, dft_t.astype(f)


def program(nc, I, out):
    const_host, where, _ = shape_constants()
    V, S, G, PE, SP = nc.vector, nc.scalar, nc.gpsimd, nc.tensor, nc.sync
    top = ExitStack()
    with top:
        def sbuf(name, shape, dt=F32, ctx=top):
            return ctx.enter_context(nc.sbuf_tensor(name, shape, dt))

        def line(name):
            return Line(top.enter_context(nc.semaphore(name)))

        vec, act, pool, pe, sp = (Queue(e, line(n)) for e, n in (
            (V, "vec_done"), (S, "act_done"), (G, "pool_done"), (PE, "pe_done"), (SP, "sp_unused")))
        engines = (vec, act, pool, pe)
        landed = [line(f"weights_landed{i}") for i in range(6)]
        high_done, split_done, used_done = line("high_done"), line("split_done"), line("used_done")
        ada_landed, ada_used = line("ada_landed"), line("ada_used")
        evac_act, evac_vec = line("evac_act"), line("evac_vec")

        bank = [top.enter_context(nc.psum_tensor(f"bank{i}", [P, 512], F32)) for i in range(8)]
        bank_free = [[] for _ in range(8)]

        ring = [sbuf(f"ring{i}", [P, HALF]) for i in range(4)]
        wh, wl = sbuf("weights_high", [P, 2, HALF], F32R), sbuf("weights_low", [P, 2, HALF], F32R)
        X = sbuf("X", [P, KC, T])
        XH, XL = sbuf("XH", [P, KC, T], F32R), sbuf("XL", [P, KC, T], F32R)
        con = sbuf("const_tables", [P, const_host.shape[1]])
        cols1, cols2 = sbuf("columns1", [P, P]), sbuf("columns2", [P, P])
        ones = sbuf("ones", [P, P])
        rstd_t = sbuf("rstd", [P, T])
        tmp = sbuf("tmp", [P, 2, T])
        sq = sbuf("squares", [P, 2, T])

        mod_t = sbuf("modulation", [P, 48, 2])
        c_silu = sbuf("c_silu", [P, KC, 2])
        ada = I["w_ada_2"][0].rearrange("(k p) n -> p k n", p=P)
        ada_slot = ring[2][:, :].rearrange("p (k n) -> p k n", k=KC)

        def const(name):
            at, n = where[name]
            return con[:, at:at + n]

        ident = const("ident")

        def join():
            for q in engines:
                q.need(vec.line.now(), act.line.now(), pool.line.now(), pe.line.now(),
                       evac_act.now(), evac_vec.now(), used_done.now(), split_done.now())

        def load(queue, ln, dst, src, after=()):
            queue.need(*after)
            queue.eng.dma_start(dst, src).then_inc(ln.sem, 16)
            ln.n += 16
            return ln.now()

        g_count = [0]

        def three_pass(out_ap, w_h, w_l, x_h, x_l, first, last):
            PE.matmul(out_ap, w_h, x_h, start=first, stop=False, skip_group_check=True)
            PE.matmul(out_ap, w_h, x_l, start=False, stop=False, skip_group_check=True)
            return PE.matmul(out_ap, w_l, x_h, start=False, stop=last, skip_group_check=True)

        def split(g, s, value, slot=None, used=None):
            slot = s if slot is None else slot
            S.wait_ge(landed[slot].sem, value)
            S.wait_ge(used_done.sem, max(g - 1, 0) if used is None else used)
            S.copy(wh[:, s, :], ring[slot][:, :]).then_inc(high_done.sem, 1)
            V.wait_ge(high_done.sem, g + 1)
            V.tensor_tensor(wl[:, s, :], ring[slot][:, :], wh[:, s, :].bitcast(F32),
                            ALU.subtract).then_inc(split_done.sem, 1)

        def modulation_step(n, static):
            if not static or n:
                G.wait_ge(ada_used.sem, n)
            G.dma_start(ada_slot, ada[:, :, bass.ds(n * P, P)]).then_inc(ada_landed.sem, 16)
            PE.wait_ge(ada_landed.sem, n * 16 + 16)
            for k in range(KC):
                t = PE.matmul(bank[7][:, bass.ds(n * 2, 2)], ada_slot[:, k, :], c_silu[:, k, :], start=k == 0,
                              stop=k == KC - 1, skip_group_check=True)
            t.then_inc(ada_used.sem, 1)

        def stream(units, src, products, evacuate=None, marks=(0, 0), banks=(0, 1), side=False):
            g0 = g_count[0]
            base = [ln.n for ln in landed]
            for b in (*banks, *([7] if side else [])):
                pe.need(*bank_free[b])

            for s in range(2):
                SP.wait_ge(split_done.sem, max(g0 + s - 1, 0))
                ap, view = src(0, s)
                SP.dma_start(view(ring[s][:, :]), ap).then_inc(landed[s].sem, 16)
            a0, v0 = evac_act.n, evac_vec.n
            for s in range(2):
                split(g0 + s, s, base[s] + 16)
                PE.wait_ge(split_done.sem, g0 + s + 1)
                products(0, s, True).then_inc(used_done.sem, 1)
            n0 = ada_used.n
            if side:
                modulation_step(n0, True)
            if units > 1:
                all_engines = [x.eng.engine for x in (vec, act, pe, sp, *([pool] if side else []))]
                with nc.Fori(1, units, 1, engines=all_engines) as i:
                    for s in range(2):
                        g = i * 2 + (g0 + s)
                        SP.wait_ge(split_done.sem, g - 1)
                        ap, view = src(i, s)
                        SP.dma_start(view(ring[s][:, :]), ap).then_inc(landed[s].sem, 16)
                    for s in range(2):
                        g = i * 2 + (g0 + s)
                        split(g, s, i * 16 + (base[s] + 16), used=g - 1)
                        if evacuate:
                            evac_act.n, evac_vec.n = (half_a, half_v) if s else (a0, v0)
                            evacuate(i - 1, s, used_done, g - 1, lambda k: (i - 1) * k)
                            half_a, half_v = evac_act.n, evac_vec.n
                        PE.wait_ge(split_done.sem, g + 1)
                        if evacuate:
                            PE.wait_ge(evac_act.sem, (i - 1) * marks[0] + half_a)
                            PE.wait_ge(evac_vec.sem, (i - 1) * marks[1] + half_v)
                        products(i, s, False).then_inc(used_done.sem, 1)
                    if side:
                        modulation_step(i + n0, False)
                if evacuate:
                    assert (half_a - a0, half_v - v0) == marks, (half_a - a0, half_v - v0)
                    evac_act.n, evac_vec.n = a0 + marks[0] * (units - 1), v0 + marks[1] * (units - 1)
            g_end = g0 + 2 * units
            g_count[0] = g_end
            used_done.n = split_done.n = high_done.n = g_end
            for s in range(2):
                landed[s].n = base[s] + 16 * units
            if evacuate:
                for s in range(2):
                    evacuate(units - 1, s, used_done, g_end - 1 + s, lambda k: 0)
            for b in banks:
                bank_free[b] = [evac_act.now(), evac_vec.now()]
            if side:
                n1 = ada_used.n = n0 + units
                ada_landed.n = 16 * n1
                bank_free[7] = [vec.do(V.tensor_copy, mod_t[:, n0:n1, :],
                                       bank[7][:, 2 * n0:2 * n1].rearrange("p (n j) -> p n j", j=2),
                                       after=[ada_used.now()])]

        def columns_src(w, width=P, base=0):
            v = w.rearrange("(k p) n -> p k n", p=P)

            def src(i, s):
                return (v[:, :, bass.ds(i * (2 * P) + (base + s * P), P)],
                        lambda r: r.rearrange("p (k n) -> p k n", k=KC))
            return src

        def rows_src(w):
            v = w.rearrange("(k p) n -> p k n", p=P)

            def src(i, s):
                return v[:, bass.ds(i * 2 + s, 1), :], lambda r: r.rearrange("p (k n) -> p k n", k=1)
            return src

        def columns_products(n, xh, xl, to=0):
            def products(i, s, first):
                w_h = wh[:, s, :].rearrange("p (k n) -> p k n", k=KC)
                w_l = wl[:, s, :].rearrange("p (k n) -> p k n", k=KC)
                for k in range(KC):
                    last = three_pass(bank[to + s][:, 0:n], w_h[:, k, :], w_l[:, k, :], xh[:, k, 0:n],
                                      xl[:, k, 0:n], k == 0, k == KC - 1)
                return last
            return products

        def rows_products(xh, xl):
            def products(i, s, first):
                w_h = wh[:, s, :].rearrange("p (c n) -> p c n", c=KC)
                w_l = wl[:, s, :].rearrange("p (c n) -> p c n", c=KC)
                for c in range(KC):
                    x_h = xh[:, bass.ds(i * 2 + s, 1), :].rearrange("p a t -> p (a t)")
                    x_l = xl[:, bass.ds(i * 2 + s, 1), :].rearrange("p a t -> p (a t)")
                    last = three_pass(bank[c][:, :], w_h[:, c, :], w_l[:, c, :], x_h, x_l,
                                      first and s == 0, False)
                return last
            return products

        def flat(tile, index, n):
            return tile[:, bass.ds(index, 1), 0:n].rearrange("p a t -> p (a t)")

        def evac_to(tile, n, base=0):
            def evacuate(i, s, ln, value, off):
                dst = flat(tile, i * 2 + (s + base), n)
                if s == 0:
                    S.wait_ge(ln.sem, value)
                    S.copy(dst, bank[0][:, 0:n]).then_inc(evac_act.sem, 1)
                    evac_act.n += 1
                else:
                    V.wait_ge(ln.sem, value)
                    V.tensor_copy(dst, bank[1][:, 0:n]).then_inc(evac_vec.sem, 1)
                    evac_vec.n += 1
            return evacuate

        def split_to(high, low, src, after, hi_bias=None):
            h = act.do(S.copy, high, src, after=after)
            return vec.do(V.tensor_tensor, low, src, high.bitcast(F32), ALU.subtract, after=[h])

        def norm_scale(src, n, after, eps=EPS, chunks=KC, b=0):
            pe.need(*bank_free[b])
            last = None
            used = [None, None]
            for k in range(chunks):
                t = act.do(S.activation, sq[:, k % 2, 0:n], src(k), ACT.Square,
                           after=[*after, *([used[k % 2]] if used[k % 2] else [])])
                last = used[k % 2] = pe.do(PE.matmul, bank[b][:, 0:n], ones[:, :], sq[:, k % 2, 0:n],
                                           start=k == 0, stop=k == chunks - 1, after=[t])
            t = vec.do(V.tensor_scalar, rstd_t[:, 0:n], bank[b][:, 0:n], 1.0 / (P * chunks), eps,
                       ALU.mult, ALU.add, after=[last])
            bank_free[b] = [t]
            t = vec.do(V.reciprocal, rstd_t[:, 0:n], rstd_t[:, 0:n], after=[t])
            return act.do(S.activation, rstd_t[:, 0:n], rstd_t[:, 0:n], ACT.Sqrt, after=[t])

        def norm_split(src, n, gain, high, low, after, shift=None):
            ready = norm_scale(lambda k: src[:, k, 0:n], n, after)
            done = [None, None]

            def scaled(k):
                return vec.do(V.scalar_tensor_tensor, tmp[:, k % 2, 0:n], src[:, k, 0:n], gain[:, k:k + 1],
                              rstd_t[:, 0:n], ALU.mult, ALU.mult,
                              after=[ready, *([done[k % 2]] if done[k % 2] else [])])
            t = scaled(0)
            for k in range(KC):
                if shift is None:
                    h = act.do(S.copy, high[:, k, 0:n], tmp[:, k % 2, 0:n], after=[t])
                else:
                    h = act.do(S.activation, high[:, k, 0:n], tmp[:, k % 2, 0:n], ACT.Identity,
                               bias=shift[:, k:k + 1], after=[t])
                if k + 1 < KC:
                    t = scaled(k + 1)
                if shift is None:
                    done[k % 2] = vec.do(V.tensor_tensor, low[:, k, 0:n], tmp[:, k % 2, 0:n],
                                         high[:, k, 0:n].bitcast(F32), ALU.subtract, after=[h])
                else:
                    done[k % 2] = vec.do(V.scalar_tensor_tensor, low[:, k, 0:n], tmp[:, k % 2, 0:n],
                                         shift[:, k:k + 1], high[:, k, 0:n].bitcast(F32), ALU.add,
                                         ALU.subtract, after=[h])

        def residual_add(M, gain, after=()):
            ready = norm_scale(lambda k: M[:, k, :], T, [vec.line.now(), act.line.now(), evac_act.now(),
                                                         evac_vec.now(), *after])
            done = [None, None]
            for k in range(KC):
                t = vec.do(V.scalar_tensor_tensor, tmp[:, k % 2, :], M[:, k, :], gain[:, k:k + 1], rstd_t[:, :],
                           ALU.mult, ALU.mult, after=[ready, *([done[k % 2]] if done[k % 2] else [])])
                done[k % 2] = pool.do(G.tensor_tensor, X[:, k, :], X[:, k, :], tmp[:, k % 2, :], ALU.add, after=[t])

        def banks_to(tile):
            for c in range(KC):
                q, op = ((act, S.copy), (vec, V.tensor_copy))[c % 2]
                bank_free[c] = [q.do(op, tile[:, c, :], bank[c][:, :], after=[used_done.now()])]

        def to_features(src, tiles, dst, after):
            for k in range(KC):
                pe.need(*bank_free[k], *after)
                for t in range(tiles):
                    tok = pe.do(PE.transpose, bank[k][:, t * P:(t + 1) * P], src[:, t, k * P:(k + 1) * P], ident)
                q, op = ((act, S.copy), (vec, V.tensor_copy))[k % 2]
                bank_free[k] = [q.do(op, dst[:, k, 0:tiles * P], bank[k][:, 0:tiles * P], after=[tok])]

        def attention(ctx, tag, heads, score, mask, sink, values, put):
            sc = sq
            pt = sbuf(f"{tag}_probs_t", [P, 2, 2, T], F32, ctx)
            small = sbuf(f"{tag}_small", [P, 2, 8], F32, ctx)
            steps = [(h, pair) for h in range(heads) for pair in range(2)]
            exp_done, sc_free, pt_free, pt_done = {}, {}, {}, {}

            def scores_and_exp(n):
                h, pair = steps[n]
                b, z = n % 2, n % 2
                pe.need(*bank_free[b])
                done = score(h, pair, bank[b])
                row = small[:, z, :]
                free = sc_free.get(n - 2, [])
                if mask is not None:
                    at, scale = sc[:, z, :], 1.0
                    done = vec.do(V.scalar_tensor_tensor, at, bank[b][:, :], SCALE, mask(pair), ALU.mult,
                                  ALU.add, after=[done, *free])
                    bank_free[b] = [done]
                else:
                    at, scale = bank[b][:, :], SCALE
                at = at.rearrange("p (a c) -> p a c", a=2)
                m = vec.do(V.tensor_reduce, row[:, 0:2], at, AX, ALU.max, after=[done, *free])
                if sink is not None:
                    m = vec.do(V.tensor_scalar, row[:, 0:2], row[:, 0:2], sink[:, h:h + 1], -1.0, ALU.max,
                               ALU.mult, after=[m])
                else:
                    m = vec.do(V.tensor_scalar, row[:, 0:2], row[:, 0:2], -SCALE, None, ALU.mult, after=[m])
                act.need(*free)
                for a in range(2):
                    e = act.do(S.activation, sc[:, z, a * 256:(a + 1) * 256], at[:, a, :], ACT.Exp,
                               bias=row[:, a:a + 1], scale=scale, accum_out=row[:, 2 + a:3 + a], after=[m])
                if mask is None:
                    bank_free[b] = [e]
                if sink is not None:
                    e = act.do(S.activation, row[:, 4:6], row[:, 0:2], ACT.Exp, bias=sink[:, h:h + 1], after=[m])
                    e = vec.do(V.tensor_tensor, row[:, 2:4], row[:, 2:4], row[:, 4:6], ALU.add, after=[e])
                e = vec.do(V.reciprocal, row[:, 2:4], row[:, 2:4], after=[e])
                for a in range(2):
                    t = vec.do(V.tensor_scalar, sc[:, z, a * 256:(a + 1) * 256], sc[:, z, a * 256:(a + 1) * 256],
                               row[:, 2 + a:3 + a], None, ALU.mult, after=[e])
                exp_done[n] = t

            def turn(n):
                h, pair = steps[n]
                b = 2 + n % 2
                pe.need(*bank_free[b], exp_done[n])
                for j in range(2):
                    for a in range(2):
                        t = pe.do(PE.transpose, bank[b][:, (2 * j + a) * P:(2 * j + a + 1) * P],
                                  sc[:, n % 2, a * 256 + j * P:a * 256 + (j + 1) * P], ident)
                sc_free[n] = [t]
                t = act.do(S.copy, pt[:, h % 2, :, pair * 256:(pair + 1) * 256],
                           bank[b][:, :].rearrange("p (j q) -> p j q", j=2), after=[t, *pt_free.get(h - 2, [])])
                bank_free[b] = [t]
                pt_done[n] = t

            def weigh(h):
                b = 4 + (h // 2) % 2
                o = DH * (h % 2)
                if h % 2 == 0:
                    pe.need(*bank_free[b])
                pe.need(pt_done[2 * h], pt_done[2 * h + 1])
                t = values(h, bank[b][o:o + DH, :], pt[:, h % 2, :, :])
                pt_free[h] = [t]
                if h % 2:
                    bank_free[b] = [put(h // 2, bank[b][:, :], t)]

            for n in range(len(steps) + 2):
                if n < len(steps):
                    scores_and_exp(n)
                if 1 <= n <= len(steps):
                    turn(n - 1)
                if n >= 3 and n % 2 == 1:
                    weigh((n - 3) // 2)

        def put_split(base):
            def put(c, src, t):
                h = act.do(S.copy, XH[:, base + c, :], src, after=[t])
                return vec.do(V.tensor_tensor, XL[:, base + c, :], src, XH[:, base + c, :].bitcast(F32),
                              ALU.subtract, after=[h])
            return put

        def memory_attention(ctx, tag, mq, mk, mv):
            def score(h, pair, dst):
                c, o = h // 2, DH * (h % 2)
                for a in range(2):
                    q = (2 * pair + a) * P
                    t = pe.do(PE.matmul, dst[:, a * 256:(a + 1) * 256], mq(c)[o:o + DH, q:q + P],
                              mk[o:o + DH, c, :], start=True, stop=True)
                return t

            def values(h, dst, pt):
                for j in range(2):
                    t = pe.do(PE.matmul, dst, mv[:, j, h * DH:(h + 1) * DH], pt[:, j, :], start=j == 0, stop=j == 1)
                return t
            attention(ctx, tag, MEM_HEADS, score, None, None, values, put_split(6))

        io, io_pool = line("inputs_landed"), line("vectors_landed")
        load(act, io, con[:, :], I["constants"])
        mem_ctx = ExitStack()
        mk = sbuf("mem_keys", [P, 2, 2, TM], F32, mem_ctx)
        mv = sbuf("mem_values", [P, 2, 2, TM], F32, mem_ctx)
        early = ExitStack()
        xin, memin = sbuf("x_tokens", [P, TT, D], F32, early), sbuf("mem_tokens", [P, 2, D], F32, early)
        rows1, rows2 = sbuf("rows1", [P, P], F32, early), sbuf("rows2", [P, P], F32, early)
        load(act, io, xin[:, :, :], I["x"][0].rearrange("(t p) d -> p t d", p=P))
        load(act, io, memin[:, :, :], I["mem"][0].rearrange("(t p) d -> p t d", p=P))

        def r8(ap):
            return ap.rearrange("(r n) -> r n", n=P)
        names1 = [("mix_pre0", I["norm_mix_pre"][0]), ("mix_pre1", I["norm_mix_pre"][1]),
                  ("mix_post0", I["norm_mix_post"][0]), ("mix_post1", I["norm_mix_post"][1]),
                  ("ffn_pre0", I["norm_ffn_pre"][0]), ("ffn_pre1", I["norm_ffn_pre"][1]),
                  ("ffn_post0", I["norm_ffn_post"][0]), ("ffn_post1", I["norm_ffn_post"][1]),
                  ("mem_norm", I["mem_norm"]), ("conv0", I["conv_w"][0, 0]), ("conv1", I["conv_w"][0, 1]),
                  ("conv2", I["conv_w"][0, 2]), ("conv3", I["conv_w"][0, 3]), ("conv_b", I["conv_b"][0]),
                  ("b_r", I["b_gate_r"][0]), ("b_i", I["b_gate_i"][0]), ("lam", I["lru_lambda"][0]),
                  ("norm_kv", I["norm_kv"])]
        names2 = [("c", I["c_2"][0]), ("c_ctx", I["c_ctx_2"]), ("b_ada", I["b_ada_2"][0]),
                  ("g_pre_mix", I["g_pre_mix_2"][0]), ("g_post_mix", I["g_post_mix_2"][0]),
                  ("g_pre_ffn", I["g_pre_ffn_2"][0]), ("g_post_ffn", I["g_post_ffn_2"][0]),
                  ("mconv0", I["conv_w_2"][0, 0]), ("mconv1", I["conv_w_2"][0, 1]),
                  ("mconv2", I["conv_w_2"][0, 2]), ("mconv_b", I["conv_b_2"][0]),
                  ("m_norm", I["mlstm_norm_w_2"][0]), ("m_skip", I["mlstm_skip_2"][0])]
        column = {}
        z = vec.do(V.memset, rows2[:, :], 0.0)
        t1 = vec.do(V.memset, ones[:, :], 1.0)
        for names, rows, cols in ((names1, rows1, cols1), (names2, rows2, cols2)):
            at = 0
            for name, ap in names:
                n = ap.shape[0] // P
                load(pool, io_pool, rows[at:at + n, :], r8(ap), after=[z])
                column[name] = cols[:, at:at + n]
                at += n
            assert at <= P
        for q in engines:
            q.need(io.now(), io_pool.now(), t1)
        for b, (rows, cols) in enumerate(((rows1, cols1), (rows2, cols2))):
            t = pe.do(PE.transpose, bank[b][:, 0:P], rows[:, :], ident)
            bank_free[b] = [vec.do(V.tensor_copy, cols[:, :], bank[b][:, 0:P], after=[t])]
        to_features(xin, TT, X, [])
        act.do(S.activation, c_silu[:, :, 0], column["c"], ACT.Silu)
        act.do(S.activation, c_silu[:, :, 1], column["c_ctx"], ACT.Silu)
        join()

        memx = sbuf("mem_features", [P, KC, TM], F32, early)
        to_features(memin, 2, memx, [])
        join()
        norm_split(memx, TM, column["mem_norm"], XH, XL, [])
        join()

        def memory_kv(l):
            w = I["w_mem_kv"][l]
            stream(1, columns_src(w), columns_products(TM, XH, XL), evac_to(mk[:, l], TM), (1, 1))

            def products(i, s, first):
                w_h = wh[:, s, :].rearrange("p (k n) -> p k n", k=KC)
                w_l = wl[:, s, :].rearrange("p (k n) -> p k n", k=KC)
                for mt in range(2):
                    for k in range(KC):
                        x_h, x_l = XH[:, k, mt * P:(mt + 1) * P], XL[:, k, mt * P:(mt + 1) * P]
                        last = three_pass(bank[s][:, mt * P:(mt + 1) * P], x_h, x_l, w_h[:, k, :], w_l[:, k, :],
                                          k == 0, k == KC - 1)
                return last

            def evacuate(i, s, ln, value, off):
                V.wait_ge(ln.sem, value)
                V.tensor_copy(mv[:, l, :, s * P:(s + 1) * P],
                              bank[s][:, 0:2 * P].rearrange("p (m n) -> p m n", m=2)).then_inc(evac_vec.sem, 1)
                evac_vec.n += 1
            stream(1, columns_src(w, base=TM), products, evacuate, (0, 2))
        memory_kv(0)
        memory_kv(1)
        join()
        early.close()

        def finish(tag, gain):
            with ExitStack() as ctx:
                M = sbuf(f"{tag}_out", [P, KC, T], F32, ctx)
                banks_to(M)
                residual_add(M, gain)
                join()

        def ffn(l):
            norm_split(X, T, column[f"ffn_pre{l}"], XH, XL, [vec.line.now(), pool.line.now()])
            join()
            ctx = ExitStack()
            HH, HL = sbuf(f"hidden_high{l}", [P, FC, T], F32R, ctx), sbuf(f"hidden_low{l}", [P, FC, T], F32R, ctx)
            sg, hid = tmp[:, 0, :], tmp[:, 1, :]
            pair = I["w_ffn_in"][l].rearrange("(k p) (h n) -> p k h n", p=P, h=2)

            def src(i, s):
                return (pair[:, :, s, bass.ds(i * P, P)], lambda r: r.rearrange("p (k n) -> p k n", k=KC))

            def evacuate(i, s, ln, value, off):
                if s == 0:
                    S.wait_ge(ln.sem, value)
                    S.wait_ge(evac_vec.sem, off(2) + evac_vec.n)
                    S.activation(sg, bank[0][:, :], ACT.Silu).then_inc(evac_act.sem, 1)
                    evac_act.n += 1
                else:
                    V.wait_ge(ln.sem, value)
                    V.wait_ge(evac_act.sem, off(2) + evac_act.n)
                    V.tensor_tensor(hid, sg, bank[1][:, :], ALU.mult).then_inc(evac_vec.sem, 1)
                    evac_vec.n += 1
                    S.wait_ge(evac_vec.sem, off(2) + evac_vec.n)
                    S.copy(flat(HH, i, T), hid).then_inc(evac_act.sem, 1)
                    evac_act.n += 1
                    V.wait_ge(evac_act.sem, off(2) + evac_act.n)
                    V.tensor_tensor(flat(HL, i, T), hid, flat(HH, i, T).bitcast(F32),
                                    ALU.subtract).then_inc(evac_vec.sem, 1)
                    evac_vec.n += 1
            stream(FC, src, columns_products(T, XH, XL), evacuate, (2, 2), side=True)
            join()
            stream(FC // 2, rows_src(I["w_ffn_out"][l]), rows_products(HH, HL), banks=range(8))
            join()
            ctx.close()
            finish(f"ffn{l}", column[f"ffn_post{l}"])

        def mix_out(tag, w, gain):
            join()
            stream(KC // 2, rows_src(w), rows_products(XH, XL), banks=range(8))
            finish(tag, gain)

        norm_split(X, T, column["mix_pre0"], XH, XL, [])
        join()
        a_ctx = ExitStack()
        proj = sbuf("proj_a", [P, 14, T], F32, a_ctx)
        stream(7, columns_src(I["w_in_a"][0]), columns_products(T, XH, XL), evac_to(proj, T), (1, 1))
        join()
        xc, gr, gi, aa = (sbuf(n, [P, 6, T], F32, a_ctx) for n in ("conv_x", "gate_r", "gate_i", "decay"))
        wgr, wgi = sbuf("w_gate_r", [P, 6, P], F32, a_ctx), sbuf("w_gate_i", [P, 6, P], F32, a_ctx)
        lgate = line("gates_landed")
        load(pool, lgate, wgr[:, :, :], I["w_gate_r"][0].rearrange("h i j -> i h j"))
        load(pool, lgate, wgi[:, :, :], I["w_gate_i"][0].rearrange("h i j -> i h j"))
        lsl = sbuf("log_sig", [P, 3, 6], F32, a_ctx)
        t = vec.do(V.scalar_tensor_tensor, lsl[:, 0, :], column["lam"], -1.0, column["lam"], ALU.mult, ALU.min)
        t = act.do(S.activation, lsl[:, 0, :], lsl[:, 0, :], ACT.Exp, after=[t])
        t = act.do(S.activation, lsl[:, 0, :], lsl[:, 0, :], ACT.Ln, bias=1.0, after=[t])
        u = vec.do(V.tensor_scalar, lsl[:, 1, :], column["lam"], 0.0, None, ALU.min)
        t = vec.do(V.tensor_tensor, lsl[:, 1, :], lsl[:, 1, :], lsl[:, 0, :], ALU.subtract, after=[t, u])
        u = vec.do(V.tensor_scalar, lsl[:, 2, :], lsl[:, 1, :], 2 * LRU_C, None, ALU.mult, after=[t])
        lam_ready = vec.do(V.tensor_scalar, lsl[:, 0, :], lsl[:, 1, :], LRU_C, None, ALU.mult, after=[t])
        tok = [vec.do(V.tensor_scalar, xc[:, c, :], proj[:, c, :], column["conv3"][:, c:c + 1],
                      column["conv_b"][:, c:c + 1], ALU.mult, ALU.add) for c in range(6)]
        for j in (2, 1, 0):
            d = 3 - j
            tok = [vec.do(V.scalar_tensor_tensor, xc[:, c, d:], proj[:, c, 0:T - d], column[f"conv{j}"][:, c:c + 1],
                          xc[:, c, d:], ALU.mult, ALU.add, after=[tok[c]]) for c in range(6)]
        sig = {}
        for c in range(6):
            for n, (w, dst, b) in enumerate(((wgr, gr, "b_r"), (wgi, gi, "b_i"))):
                k = (2 * c + n) % 4
                t = pe.do(PE.matmul, bank[k][:, :], w[:, c, :], xc[:, c, :], start=True, stop=True,
                          after=[lgate.now(), tok[c], *bank_free[k]])
                sig[n, c] = act.do(S.activation, dst[:, c, :], bank[k][:, :], ACT.Sigmoid,
                                   bias=column[b][:, c:c + 1], after=[t])
                bank_free[k] = [sig[n, c]]
        ta = [act.do(S.activation, aa[:, c, :], gr[:, c, :], ACT.Exp, scale=lsl[:, 0, c:c + 1],
                     after=[sig[0, c], lam_ready]) for c in range(6)]
        tb = [act.do(S.activation, gr[:, c, :], gr[:, c, :], ACT.Exp, scale=lsl[:, 2, c:c + 1],
                     after=[ta[c]]) for c in range(6)]
        tx = [vec.do(V.tensor_tensor, gi[:, c, :], gi[:, c, :], xc[:, c, :], ALU.mult, after=[sig[1, c]])
              for c in range(6)]
        tb = [vec.do(V.tensor_scalar, gr[:, c, :], gr[:, c, :], 1.0, -1.0, ALU.min, ALU.mult, after=[tb[c]])
              for c in range(6)]
        tb = [act.do(S.activation, gr[:, c, :], gr[:, c, :], ACT.Sqrt, bias=1.0, after=[tb[c]]) for c in range(6)]
        t = vec.do(V.memset, gr[:, :, 0:1], 1.0, after=[tb[-1]])
        tx = [vec.do(V.tensor_tensor, gi[:, c, :], gi[:, c, :], gr[:, c, :], ALU.mult, after=[t, tx[c]])
              for c in range(6)]
        th = [vec.do(V.tensor_tensor_scan, xc[:, c, :], aa[:, c, :], gi[:, c, :], 0.0, ALU.mult, ALU.add,
                     after=[tx[c], ta[c]]) for c in range(6)]
        tg = [act.do(S.activation, proj[:, 6 + c, :], proj[:, 6 + c, :], ACT.Gelu_apprx_tanh) for c in range(6)]
        for c in range(6):
            t = vec.do(V.tensor_tensor, xc[:, c, :], xc[:, c, :], proj[:, 6 + c, :], ALU.mult, after=[th[c], tg[c]])
            split_to(XH[:, c, :], XL[:, c, :], xc[:, c, :], [t])
        memory_attention(a_ctx, "mem0", lambda c: proj[:, 12 + c, :], mk[:, 0], mv[:, 0])
        join()
        a_ctx.close()
        mix_out("mix0", I["w_out"][0], column["mix_post0"])
        ffn(0)

        b_ctx = ExitStack()
        KT = sbuf("keys", [P, KV_HEADS, T], F32, b_ctx)
        VS = sbuf("values", [P, TT, KV_HEADS * DH], F32, b_ctx)
        projb = sbuf("proj_b", [P, KC, T], F32, b_ctx)
        rot = sbuf("rotated", [P, 2, T], F32, b_ctx)
        sinkc = sbuf("sinks", [P, Q_HEADS], F32, b_ctx)
        sinkr = sbuf("sink_row", [1, Q_HEADS], F32, b_ctx)
        lsink = line("sink_landed")
        load(pool, lsink, sinkr[:, :], I["sinks"][0:1, :])
        t = pe.do(PE.matmul, bank[7][:, 0:Q_HEADS], ones[0:1, :], sinkr[:, :], start=True, stop=True,
                  after=[lsink.now(), *bank_free[7]])
        bank_free[7] = [vec.do(V.tensor_copy, sinkc[:, :], bank[7][:, 0:Q_HEADS], after=[t])]
        norm_split(X, T, column["norm_kv"], XH, XL, [])
        join()

        def key_evac(i, s, ln, value, off):
            eng, op, ev = ((S, S.copy, evac_act), (V, V.tensor_copy, evac_vec))[s]
            eng.wait_ge(ln.sem, value)
            for a in range(2):
                for to in (0, DH):
                    op(KT[to:to + DH, 2 * s + a, :], bank[s][a * DH:(a + 1) * DH, :]).then_inc(ev.sem, 1)
                    ev.n += 1
        stream(1, columns_src(I["w_kv_shared"]), columns_products(T, XH, XL), key_evac, (4, 4))

        def value_products(i, s, first):
            w_h = wh[:, s, :].rearrange("p (k n) -> p k n", k=KC)
            w_l = wl[:, s, :].rearrange("p (k n) -> p k n", k=KC)
            for t4 in range(TT):
                for k in range(KC):
                    x_h, x_l = XH[:, k, t4 * P:(t4 + 1) * P], XL[:, k, t4 * P:(t4 + 1) * P]
                    last = three_pass(bank[s][:, t4 * P:(t4 + 1) * P], x_h, x_l, w_h[:, k, :], w_l[:, k, :],
                                      k == 0, k == KC - 1)
            return last

        def value_evac(i, s, ln, value, off):
            V.wait_ge(ln.sem, value)
            V.tensor_copy(VS[:, :, s * P:(s + 1) * P],
                          bank[s][:, :].rearrange("p (m n) -> p m n", m=TT)).then_inc(evac_vec.sem, 1)
            evac_vec.n += 1
        stream(1, columns_src(I["w_kv_shared"], base=KV_HEADS * DH), value_products, value_evac, (0, 2))
        join()

        def rope(chunks):
            for n, x in enumerate(chunks):
                b = 2 + n % 2
                t = pe.do(PE.matmul, bank[b][:, :], const("swap"), x, start=True, stop=True, after=[*bank_free[b]])
                u = vec.do(V.tensor_tensor, rot[:, n % 2, :], bank[b][:, :], const("rope_sin"), ALU.mult, after=[t])
                bank_free[b] = [u]
                w = vec.do(V.tensor_tensor, x, x, const("rope_cos"), ALU.mult, after=[t])
                vec.do(V.tensor_tensor, x, x, rot[:, n % 2, :], ALU.add, after=[u, w])
        rope([KT[:, g, :] for g in range(KV_HEADS)])

        norm_split(X, T, column["mix_pre1"], XH, XL, [])
        join()
        stream(4, columns_src(I["w_in_b"][0]), columns_products(T, XH, XL), evac_to(projb, T), (1, 1), side=True)
        join()
        rope([projb[:, c, :] for c in range(6)])
        join()

        def window_score(h, pair, dst):
            g, c, o = h // (Q_HEADS // KV_HEADS), h // 2, DH * (h % 2)
            for a in range(2):
                blk = 2 * pair + a
                q = projb[o:o + DH, c, blk * P:(blk + 1) * P]
                if blk:
                    t = pe.do(PE.matmul, dst[:, a * 256:(a + 1) * 256], q, KT[o:o + DH, g, (blk - 1) * P:(blk + 1) * P],
                              start=True, stop=True)
                else:
                    for j in range(2):
                        t = pe.do(PE.matmul, dst[:, j * P:(j + 1) * P], q, KT[o:o + DH, g, 0:P], start=True, stop=True)
            return t

        def window_values(h, dst, pt):
            g = h // (Q_HEADS // KV_HEADS)
            for blk in range(TT):
                for j in range(2):
                    v = VS[:, max(blk - 1 + j, 0), g * DH:(g + 1) * DH]
                    t = pe.do(PE.matmul, dst[:, blk * P:(blk + 1) * P], v, pt[:, j, blk * P:(blk + 1) * P],
                              start=j == 0, stop=j == 1, skip_group_check=True)
            return t
        win = const("window")
        attention(b_ctx, "swa", Q_HEADS, window_score, lambda pair: win[:, pair * 512:(pair + 1) * 512], sinkc,
                  window_values, put_split(0))
        memory_attention(b_ctx, "mem1", lambda c: projb[:, 6 + c, :], mk[:, 1], mv[:, 1])
        join()
        b_ctx.close()
        mix_out("mix1", I["w_out"][1], column["mix_post1"])
        ffn(1)
        mem_ctx.close()
        for k in range(KC):
            x = X[:, k, :].rearrange("p (r c) -> p r c", c=64)
            if k < 4:
                e = const("emb_row")[:, 8 * k:8 * k + 8].unsqueeze(2).broadcast_to([P, 8, 64])
            else:
                e = const("emb_col")[:, 64 * (k - 4):64 * (k - 3)].unsqueeze(1).broadcast_to([P, 8, 64])
            vec.do(V.tensor_tensor, x, x, e, ALU.add)

        mod = sbuf("modulation_biased", [P, 2, 48])
        gains = sbuf("gains", [P, 5, KC])
        join()
        for j in range(2):
            t = vec.do(V.tensor_tensor, mod[:, j, :], mod_t[:, :, j], column["b_ada"], ALU.add)

        def section(j, n):
            return mod[:, j, 8 * n:8 * n + 8]
        SHIFT1, SCALE1, GATE1, SHIFT2, SCALE2, GATE2 = range(6)
        for n, (j, sec, add, g) in enumerate(((0, SCALE1, 1.0, "g_pre_mix"), (1, SCALE1, 1.0, "g_pre_mix"),
                                              (0, GATE1, 0.0, "g_post_mix"), (0, SCALE2, 1.0, "g_pre_ffn"),
                                              (0, GATE2, 0.0, "g_post_ffn"))):
            vec.do(V.scalar_tensor_tensor, gains[:, n, :], section(j, sec), add, column[g], ALU.add, ALU.mult,
                   after=[t])
        PRE_MIX, PRE_MIX_CTX, POST_MIX, PRE_FFN, POST_FFN = (gains[:, n, :] for n in range(5))
        join()

        m_ctx = ExitStack()
        TALL = TM + T
        zu = sbuf("z_and_u", [P, KC, T], F32, m_ctx)
        xm = sbuf("x_m", [P, MH, TALL], F32, m_ctx)
        ac = sbuf("act", [P, MH, TALL], F32, m_ctx)
        with ExitStack() as p_ctx:
            ctx_x = sbuf("ctx_features", [P, KC, TM], F32, p_ctx)
            CH, CL = sbuf("ctx_high", [P, KC, TM], F32R, p_ctx), sbuf("ctx_low", [P, KC, TM], F32R, p_ctx)
            ctx_tok = sbuf("ctx_tokens", [P, 2, D], F32, p_ctx)
            lctx = line("ctx_landed")
            load(act, lctx, ctx_tok[:, :, :], I["ctx_2"][0].rearrange("(t p) d -> p t d", p=P))
            to_features(ctx_tok, 2, ctx_x, [lctx.now()])
            join()
            norm_split(ctx_x, TM, PRE_MIX_CTX, CH, CL, [], shift=section(1, SHIFT1))
            join()
            norm_split(X, T, PRE_MIX, XH, XL, [], shift=section(0, SHIFT1))
            join()

            def both_products(i, s, first):
                columns_products(T, XH, XL)(i, s, first)
                return columns_products(TM, CH, CL, to=2)(i, s, first)

            def both_evac(i, s, ln, value, off):
                eng, op, ev = ((S, S.copy, evac_act), (V, V.tensor_copy, evac_vec))[s]
                eng.wait_ge(ln.sem, value)
                for b, lo, n in ((s, TM, T), (2 + s, 0, TM)):
                    dst = xm[:, bass.ds(i * 2 + s, 1), lo:lo + n].rearrange("p a t -> p (a t)")
                    op(dst, bank[b][:, 0:n]).then_inc(ev.sem, 1)
                    ev.n += 1
            stream(2, columns_src(I["w_in_2"][0]), both_products, both_evac, (2, 2), banks=range(4))
            stream(4, columns_src(I["w_in_2"][0], base=MH * P), columns_products(T, XH, XL), evac_to(zu, T), (1, 1))
            join()

        with ExitStack() as f_ctx:
            zt = sbuf("u_mixed", [P, TT, 4, 2 * P], F32, f_ctx)
            dft = sbuf("dft_t", [P, TT, 2 * T], F32, f_ctx)
            wf, cw = sbuf("w_fourier", [P, 4, P], F32, f_ctx), sbuf("dft_w", [P, 4, 2 * P], F32, f_ctx)
            lf = line("fourier_landed")
            load(act, lf, dft[:, :, :], I["dft_t"].rearrange("(t p) n -> p t n", p=P))
            load(act, lf, wf[:, :, :], I["w_fourier_2"][0].rearrange("g c d -> c g d"))
            for g in range(4):
                for j in range(2):
                    t = pe.do(PE.matmul, bank[g][:, j * P:(j + 1) * P], const("dft_c")[:, j * P:(j + 1) * P], wf[:, g, :],
                              start=True, stop=True, after=[lf.now(), *bank_free[g]])
                bank_free[g] = [vec.do(V.tensor_copy, cw[:, g, :], bank[g][:, 0:2 * P], after=[t])]
            for t4 in range(TT):
                for g in range(4):
                    b = 4 + (2 * t4 + g // 2) % 4
                    t = pe.do(PE.matmul, bank[b][:, (g % 2) * 256:(g % 2 + 1) * 256], zu[:, 4 + g, t4 * P:(t4 + 1) * P],
                              cw[:, g, :], start=True, stop=True, after=[vec.line.now(), *bank_free[b]])
                    if g % 2:
                        q, op = ((act, S.copy), (vec, V.tensor_copy))[g // 2]
                        bank_free[b] = [q.do(op, zt[:, t4, g - 1:g + 1, :],
                                             bank[b][:, :].rearrange("p (g n) -> p g n", g=2), after=[t])]
            join()
            for g in range(4):
                pe.need(*bank_free[g])
                for t4 in range(TT):
                    for j in range(2):
                        t = pe.do(PE.matmul, bank[g][:, :], zt[:, t4, g, j * P:(j + 1) * P], dft[:, t4, j * T:(j + 1) * T],
                                  start=t4 + j == 0, stop=t4 + j == TT)
                bank_free[g] = [put_split(4)(g, bank[g][:, :], t)]
            join()

        seg = ((0, TM), (TM, T))
        for c in range(MH):
            for lo, n in seg:
                a, x = ac[:, c, lo:lo + n], xm[:, c, lo:lo + n]
                t = vec.do(V.tensor_scalar, a, x, column["mconv1"][:, c:c + 1], column["mconv_b"][:, c:c + 1],
                           ALU.mult, ALU.add)
                t = vec.do(V.scalar_tensor_tensor, a[:, 1:], x[:, :n - 1], column["mconv0"][:, c:c + 1], a[:, 1:],
                           ALU.mult, ALU.add, after=[t])
                t = vec.do(V.scalar_tensor_tensor, a[:, :n - 1], x[:, 1:], column["mconv2"][:, c:c + 1], a[:, :n - 1],
                           ALU.mult, ALU.add, after=[t])
            act.do(S.activation, ac[:, c, :], ac[:, c, :], ACT.Silu, after=[t])
        act.do(S.activation, zu[:, 0:MH, :], zu[:, 0:MH, :], ACT.Silu)
        join()

        wb = sbuf("w_blocks", [P, 3, MH, 4], F32, m_ctx)
        bd = sbuf("w_diagonal", [P, 3, MH, P], F32, m_ctx)
        qf, kf = sbuf("q_features", [P, MH, TALL], F32, m_ctx), sbuf("k_features", [P, MH, TALL], F32, m_ctx)
        gi, lfr = sbuf("gate_in", [ROWS, TALL], F32, m_ctx), sbuf("gate_forget", [ROWS, TALL], F32, m_ctx)
        mx, ks = sbuf("running_max", [ROWS, TALL], F32, m_ctx), sbuf("key_scale", [ROWS, TALL], F32, m_ctx)
        wr, em = sbuf("carried", [ROWS, T], F32, m_ctx), sbuf("floor", [ROWS, T], F32, m_ctx)
        g_ctx = ExitStack()
        wif = sbuf("w_if", [P, 12, 100], F32, g_ctx)
        vtmp = sbuf("v_features", [P, TALL], F32, g_ctx)
        bif = sbuf("b_if", [ROWS, 2], F32, g_ctx)
        lb, lw = line("blocks_landed"), line("gate_weights_landed")
        for n, name in enumerate(("w_q_2", "w_k_2", "w_v_2")):
            load(act, lb, wb[:, n], I[name][0].rearrange("(c n) i o -> (n i) c o", c=MH))
        t = vec.do(V.memset, wif[:, :, :], 0.0)
        t = vec.do(V.memset, bif[:, :], 0.0)
        for d, (w, b) in enumerate((("w_if_fwd_2", "b_if_fwd_2"), ("w_if_bwd_2", "b_if_bwd_2"))):
            for part in range(2):
                lo = 64 * part + 32 * d
                load(act, lw, wif[:, :, lo:lo + 4],
                     I[w][0].rearrange("(j p) g -> p j g", p=P)[:, :, 4 * part:4 * part + 4], after=[t])
                load(act, lw, bif[32 * d:32 * d + 4, part:part + 1],
                     I[b][0, 4 * part:4 * part + 4].rearrange("(h o) -> h o", o=1))
        for n in range(3):
            for c in range(MH):
                t = vec.do(V.tensor_tensor, bd[:, n, c, :].rearrange("p (n o) -> p n o", o=4),
                           wb[:, n, c, :].unsqueeze(1).broadcast_to([P, 32, 4]),
                           const("quad").unsqueeze(2).broadcast_to([P, 32, 4]), ALU.mult, after=[lb.now()])
        pe.need(t, lw.now(), *bank_free[6], *bank_free[7])
        vfree = []
        for c in range(MH):
            for n in range(3):
                src = xm if n == 2 else ac
                dst = (qf[:, c, :], kf[:, c, :], vtmp[:, :])[n]
                b = 2 * ((3 * c + n) % 3)
                pe.need(*bank_free[b], *bank_free[b + 1])
                pe.do(PE.matmul, bank[b][:, :], bd[:, n, c, :], src[:, c, TM:], start=True, stop=True)
                t = pe.do(PE.matmul, bank[b + 1][:, 0:TM], bd[:, n, c, :], src[:, c, 0:TM], start=True, stop=True)
                free = vfree if n == 2 else []
                ta = act.do(S.copy, dst[:, TM:], bank[b][:, :], after=[t, *free])
                tb = vec.do(V.tensor_copy, dst[:, 0:TM], bank[b + 1][:, 0:TM], after=[t, *free])
                bank_free[b], bank_free[b + 1] = [ta], [tb]
                pe.need(ta, tb)
                w = wif[:, MH * n + c, :]
                pe.do(PE.matmul, bank[6][0:100, :], w, dst[:, TM:], start=c + n == 0, stop=c + n == 5,
                      skip_group_check=True)
                gates = pe.do(PE.matmul, bank[7][0:100, 0:TM], w, dst[:, 0:TM], start=c + n == 0, stop=c + n == 5,
                              skip_group_check=True)
                if n == 2:
                    vfree = [gates]
        for b, lo, n in ((6, TM, T), (7, 0, TM)):
            vec.do(V.tensor_scalar, gi[:, lo:lo + n], bank[b][0:ROWS, 0:n], bif[:, 0:1], None, ALU.add, after=[gates])
            t = vec.do(V.tensor_copy, lfr[:, lo:lo + n], bank[b][64:64 + ROWS, 0:n])
            bank_free[b] = [t]
        t = vec.do(V.tensor_scalar, lfr[:, :], lfr[:, :], bif[:, 1:2], None, ALU.add, after=[t])
        t = vec.do(V.scalar_tensor_tensor, ks[:, :], lfr[:, :], -1.0, lfr[:, :], ALU.mult, ALU.min, after=[t])
        t = act.do(S.activation, ks[:, :], ks[:, :], ACT.Exp, after=[t])
        t = act.do(S.activation, ks[:, :], ks[:, :], ACT.Ln, bias=1.0, after=[t])
        t = vec.do(V.scalar_tensor_tensor, lfr[:, :], lfr[:, :], 0.0, ks[:, :], ALU.min, ALU.subtract, after=[t])
        join()
        g_ctx.close()

        m0, nml, dec = (sbuf(n, [ROWS, NCH], F32, m_ctx) for n in ("m_start", "minus_m_last", "chunk_decay"))
        rcol, kcol = sbuf("r_columns", [P, NCH, ROWS], F32, m_ctx), sbuf("k_columns", [P, NCH, ROWS], F32, m_ctx)
        decb = sbuf("decay_columns", [P, 2 * MH, NCH], F32, m_ctx)
        order = ([0, 1, 2, 3, 4, 5], [1, 0, 5, 4, 3, 2])
        vec.do(V.memset, mx[:, :], 0.0)
        vec.do(V.memset, nml[:, :], 0.0)
        vec.do(V.memset, m0[:, :], 0.0)

        def in_order(tile, d, ch):
            a = tile[32 * d:32 * d + MH, ch * P:(ch + 1) * P]
            return a[:, ::-1] if d else a
        for ch in range(NCH):
            for d in range(2):
                t = vec.do(V.tensor_tensor_scan, in_order(lfr, d, ch), ones[32 * d:32 * d + MH, :],
                           in_order(lfr, d, ch), 0.0, ALU.mult, ALU.add)
        t = vec.do(V.tensor_tensor, gi[:, :], gi[:, :], lfr[:, :], ALU.subtract, after=[t])
        tl = [t, t]
        for n in range(NCH):
            for d in range(2):
                rows = slice(32 * d, 32 * d + MH)
                ch = order[d][n]
                end = ch * P if d else (ch + 1) * P - 1
                t = vec.do(V.tensor_tensor_scan, in_order(mx, d, ch), in_order(gi, d, ch), in_order(gi, d, ch),
                           m0[rows, ch:ch + 1], ALU.max, ALU.max, after=[tl[d]])
                vec.do(V.tensor_scalar, nml[rows, ch:ch + 1], mx[rows, end:end + 1], -1.0, None, ALU.mult, after=[t])
                if n + 1 < NCH:
                    nxt = order[d][n + 1]
                    tl[d] = vec.do(V.tensor_tensor, m0[rows, nxt:nxt + 1], mx[rows, end:end + 1],
                                   lfr[rows, end:end + 1], ALU.add, after=[t])
        join()
        vec.do(V.tensor_tensor, em[:, :], lfr[:, TM:], mx[:, TM:], ALU.add)
        act.do(S.activation, em[:, :], em[:, :], ACT.Exp, scale=-1.0, after=[vec.line.now()])
        for ch in range(NCH):
            act.do(S.activation, ks[:, ch * P:(ch + 1) * P], gi[:, ch * P:(ch + 1) * P], ACT.Exp, bias=nml[:, ch:ch + 1])
            if ch >= CTX_CH:
                act.do(S.activation, wr[:, (ch - 2) * P:(ch - 1) * P], mx[:, ch * P:(ch + 1) * P], ACT.Exp,
                       bias=m0[:, ch:ch + 1], scale=-1.0)
        t = vec.do(V.tensor_tensor, dec[:, :], m0[:, :], nml[:, :], ALU.add)
        act.do(S.activation, dec[:, :], dec[:, :], ACT.Exp, after=[t])
        join()
        for b, (rows, cols) in enumerate(((gi, rcol), (ks, kcol))):
            for ch in range(NCH):
                t = pe.do(PE.transpose, bank[b][:, ch * ROWS:(ch + 1) * ROWS], rows[:, ch * P:(ch + 1) * P],
                          ident[0:ROWS, 0:ROWS])
            vec.do(V.tensor_copy, cols[:, :, :], bank[b][:, 0:NCH * ROWS].rearrange("p (c r) -> p c r", c=NCH), after=[t])
        sel = const("sel").rearrange("p (j n) -> p j n", n=P)
        for j in range(2 * MH):
            t = pe.do(PE.matmul, bank[2][:, j * NCH:(j + 1) * NCH], sel[0:ROWS, j, :], dec[:, :], start=True, stop=True)
        vec.do(V.tensor_copy, decb[:, :, :], bank[2][:, 0:2 * MH * NCH].rearrange("p (j c) -> p j c", j=2 * MH), after=[t])
        join()

        ktok = sbuf("k_tokens", [P, NCH, P], F32, m_ctx)
        vtok = sbuf("v_tokens", [P, NCH, P + 1], F32, m_ctx)
        state = sbuf("state", [P, NCH, P + 1], F32, m_ctx)
        kw = sbuf("k_weighted", [P, 2, P], F32, m_ctx)
        hsum = zu[:, MH, :]
        wgt, sco, qw, flo = sq[:, 0, :], sq[:, 1, :], tmp[:, 0, :], tmp[:, 1, :]
        masks = (const("fwd_mask"), const("bwd_mask"))
        vec.do(V.memset, vtok[:, :, P:P + 1], 1.0)
        for h in range(MH):
            for n, (src, tile) in enumerate(((ac, ktok), (xm, vtok))):
                for half in range(2):
                    b = 4 + 2 * n + half
                    cnt = 4 if half == 0 else 2
                    for c in range(cnt):
                        ch = 4 * half + c
                        t = pe.do(PE.matmul, bank[b][:, c * P:(c + 1) * P], src[:, h, ch * P:(ch + 1) * P],
                                  bd[:, 1 + n, h, :], start=True, stop=True)
                    q, op = ((act, S.copy), (vec, V.tensor_copy))[half]
                    q.do(op, tile[:, 4 * half:4 * half + cnt, 0:P],
                         bank[b][:, 0:cnt * P].rearrange("p (c n) -> p c n", c=cnt), after=[t])
            join()
            for d in range(2):
                j, row = MH * d + h, 32 * d + h
                used = [[], []]
                for n in range(NCH - 1):
                    a, b = order[d][n], order[d][n + 1]
                    t = act.do(S.activation, kw[:, n % 2, :], ktok[:, a, :], ACT.Copy, scale=kcol[:, a, row:row + 1],
                               after=used[n % 2])
                    t = pe.do(PE.matmul, bank[6 + n % 2][:, 0:P + 1], kw[:, n % 2, :], vtok[:, a, :], start=True,
                              stop=True, after=[t, *([states[n - 2]] if n >= 2 else [])])
                    used[n % 2] = [t]
                    if n == 0:
                        states = [vec.do(V.tensor_copy, state[:, b, :], bank[6][:, 0:P + 1], after=[t])]
                    else:
                        states.append(vec.do(V.scalar_tensor_tensor, state[:, b, :], state[:, a, :], decb[:, j, a:a + 1],
                                             bank[6 + n % 2][:, 0:P + 1], ALU.mult, ALU.add, after=[t, states[-1]]))
                tm = pe.do(PE.matmul, bank[0][:, :], sel[0:ROWS, j, :], mx[:, TM:], start=True, stop=True)
                tw = pe.do(PE.matmul, bank[1][:, :], sel[0:ROWS, j, :], wr[:, :], start=True, stop=True)
                tf = pe.do(PE.matmul, bank[2][:, :], sel[0:ROWS, j, :], em[:, :], start=True, stop=True)
                for ch in range(TT):
                    lo = TM + ch * P
                    ts = pe.do(PE.matmul, bank[3][:, ch * P:(ch + 1) * P], kf[:, h, lo:lo + P], qf[:, h, lo:lo + P],
                               start=True, stop=True)
                t = vec.do(V.scalar_tensor_tensor, wgt.rearrange("p (c t) -> p c t", c=TT),
                           bank[0][:, :].rearrange("p (c t) -> p c t", c=TT), -1.0,
                           masks[d].unsqueeze(1).broadcast_to([P, TT, P]), ALU.mult, ALU.add, after=[tm])
                for ch in range(TT):
                    te = act.do(S.activation, wgt[:, ch * P:(ch + 1) * P], wgt[:, ch * P:(ch + 1) * P], ACT.Exp,
                                bias=rcol[:, CTX_CH + ch, row:row + 1], after=[t])
                tq = vec.do(V.scalar_tensor_tensor, qw, qf[:, h, TM:], MSCALE, bank[1][:, :], ALU.mult, ALU.mult,
                            after=[tw])
                tsc = vec.do(V.scalar_tensor_tensor, sco, bank[3][:, :], MSCALE, wgt, ALU.mult, ALU.mult,
                             after=[ts, te])
                pe.need(tq, tsc, *states)
                for ch in range(TT):
                    cols = slice(ch * P, (ch + 1) * P)
                    st = state[:, CTX_CH + ch, :]
                    pe.do(PE.matmul, bank[4][:, cols], vtok[:, CTX_CH + ch, 0:P], sco[:, cols], start=True, stop=False)
                    pe.do(PE.matmul, bank[4][:, cols], st[:, 0:P], qw[:, cols], start=False, stop=True)
                    pe.do(PE.matmul, bank[5][:, cols], ones[:, :], sco[:, cols], start=True, stop=False)
                    t = pe.do(PE.matmul, bank[5][:, cols], st[:, P:P + 1].broadcast_to([P, P]), qw[:, cols],
                              start=False, stop=True)
                t = act.do(S.activation, flo, bank[5][:, :], ACT.Abs, after=[t])
                t = vec.do(V.tensor_tensor, flo, flo, bank[2][:, :], ALU.max, after=[t, tf])
                t = vec.do(V.reciprocal, flo, flo, after=[t])
                if d == 0:
                    vec.do(V.tensor_tensor, hsum[:, :], flo, bank[4][:, :], ALU.mult, after=[t])
                else:
                    t = vec.do(V.tensor_tensor, flo, flo, bank[4][:, :], ALU.mult, after=[t])
                    vec.do(V.tensor_tensor, hsum[:, :], hsum[:, :], flo, ALU.add, after=[t])
                join()
            t = pe.do(PE.matmul, bank[1][:, :], ones[:, :], hsum[:, :], start=True, stop=True)
            t = vec.do(V.scalar_tensor_tensor, hsum[:, :], bank[1][:, :], -1.0 / P, hsum[:, :], ALU.mult, ALU.add,
                       after=[t])
            t = norm_scale(lambda k: hsum[:, :], T, [t], chunks=1)
            t = vec.do(V.scalar_tensor_tensor, hsum[:, :], hsum[:, :], column["m_norm"][:, h:h + 1], rstd_t[:, :],
                       ALU.mult, ALU.mult, after=[t])
            t = vec.do(V.scalar_tensor_tensor, hsum[:, :], ac[:, h, TM:], column["m_skip"][:, h:h + 1], hsum[:, :],
                       ALU.mult, ALU.add, after=[t])
            t = vec.do(V.tensor_tensor, hsum[:, :], hsum[:, :], zu[:, h, :], ALU.mult, after=[t])
            split_to(XH[:, h, :], XL[:, h, :], hsum[:, :], [t])
            join()
        m_ctx.close()
        mix_out("mix2", I["w_out_2"][0], POST_MIX)

        r_ctx = ExitStack()
        wts = sbuf("pair_weights", [P, 2, TT])
        slots_u = sbuf("pair_slots", [P, 2, TT], U32)
        etab_u = sbuf("block_expert", [P, BLOCKS], U32)
        h2d = nc.dram_tensor("h2_tokens", (T, D), F32, kind="Internal").ap()
        idxd = nc.dram_tensor("slot_token", (BLOCKS * P, 1), U32, kind="Internal").ap()
        yd = nc.dram_tensor("slot_output", (BLOCKS * P, D), F32, kind="Internal").ap()
        H2 = sbuf("h2", [P, KC, T], F32, r_ctx)
        h2t = sbuf("h2_tok", [P, TT, D], F32, r_ctx)
        wrt, brow = sbuf("w_router", [P, KC, 20], F32, r_ctx), sbuf("b_router", [1, 20], F32, r_ctx)
        zero_u = sbuf("zero_slots", [P, BLOCKS], U32, r_ctx)
        lr, lz = line("router_landed"), line("slots_zeroed")
        load(act, lr, wrt[:, :, 0:4], I["w_router_group_2"][0].rearrange("(k p) n -> p k n", p=P))
        load(act, lr, wrt[:, :, 4:20], I["w_router_expert_2"][0].rearrange("(k p) n -> p k n", p=P))
        load(act, lr, brow[:, 0:4], I["b_router_group_2"][0:1, :])
        load(act, lr, brow[:, 4:20], I["b_router_expert_2"][0:1, :])
        t = vec.do(V.memset, zero_u[:, :], 0)
        load(act, lz, idxd.rearrange("(p b) o -> p (b o)", p=P), zero_u[:, :], after=[t])
        ready = norm_scale(lambda k: X[:, k, :], T, [])
        for k in range(KC):
            t = vec.do(V.scalar_tensor_tensor, H2[:, k, :], X[:, k, :], PRE_FFN[:, k:k + 1], rstd_t[:, :], ALU.mult,
                       ALU.mult, after=[ready])
            act.do(S.activation, H2[:, k, :], H2[:, k, :], ACT.Identity, bias=section(0, SHIFT2)[:, k:k + 1], after=[t])
        join()
        for t4 in range(TT):
            for k in range(KC):
                t = pe.do(PE.matmul, bank[0][:, t4 * 20:t4 * 20 + 20], H2[:, k, t4 * P:(t4 + 1) * P], wrt[:, k, :],
                          start=k == 0, stop=False, after=[lr.now()])
            logits = pe.do(PE.matmul, bank[0][:, t4 * 20:t4 * 20 + 20], ones[0:1, :], brow[:, :], start=False, stop=True)
        for t4 in range(TT):
            for half in range(2):
                b = 1 + (2 * t4 + half) % 6
                pe.need(*bank_free[b])
                for c in range(4):
                    k = 4 * half + c
                    t = pe.do(PE.transpose, bank[b][:, c * P:(c + 1) * P], H2[:, k, t4 * P:(t4 + 1) * P], ident)
                q, op = ((act, S.copy), (vec, V.tensor_copy))[half]
                bank_free[b] = [q.do(op, h2t[:, t4, half * 512:(half + 1) * 512], bank[b][:, :], after=[t])]
        lh2 = line("h2_stored")
        load(act, lh2, h2d.rearrange("(t p) d -> p t d", p=P), h2t[:, :, :], after=[vec.line.now(), act.line.now()])

        small = {}

        def sm(name, *shape):
            small[name] = sbuf(f"r_{name}", [P, *shape], F32, r_ctx)
            return small[name]

        def seq(op, *args, **kw):
            return vec.do(op, *args, after=[vec.line.now(), act.line.now(), pe.line.now()], **kw)

        def bc(ap, *shape):
            return ap.broadcast_to([P, *shape])
        lg, el = sm("logits", TT, 20), sm("chosen", TT, PER)
        g1, pen = sm("max", TT, 1), sm("penalty", TT, 4)
        ohg, oh1, oh2 = sm("group", TT, 4), sm("first", TT, 4), sm("second", TT, 4)
        e4, prod = sm("exp", TT, 4), sm("product", TT, 4, 4)
        m1, m2, psel = sm("m1", TT, 1), sm("m2", TT, 1), sm("psel", TT, 1)
        A = [sm("pair1", TT, NE), sm("pair2", TT, NE)]
        asum, slot = sm("pairs", TT, NE), sm("slot", TT, NE)
        cnt, nb, inc, st_ = sm("count", NE), sm("blocks", NE), sm("blocks_to", NE), sm("start", NE)
        etf, cmpb = sm("expert_of", BLOCKS), sm("compare", BLOCKS, NE)
        seq(V.tensor_copy, lg[:, :, :], bank[0][:, 0:80].rearrange("p (t n) -> p t n", t=TT))
        iota4 = const("iota")[:, 0:4].unsqueeze(1).broadcast_to([P, TT, 4])

        def first_max(onehot, x, m):
            seq(V.tensor_reduce, m[:, :, 0], x, AX, ALU.max)
            seq(V.tensor_tensor, pen[:, :, :], x, bc(m[:, :, :], TT, 4), ALU.is_lt)
            seq(V.scalar_tensor_tensor, pen[:, :, :], pen[:, :, :], 100.0, iota4, ALU.mult, ALU.add)
            seq(V.tensor_reduce, g1[:, :, 0], pen[:, :, :], AX, ALU.min)
            seq(V.tensor_tensor, onehot[:, :, :], iota4, bc(g1[:, :, :], TT, 4), ALU.is_equal)
        first_max(ohg, lg[:, :, 0:4], m1)
        seq(V.tensor_tensor, e4[:, :, :], lg[:, :, 0:4], bc(m1[:, :, :], TT, 4), ALU.subtract)
        act.do(S.activation, e4[:, :, :], e4[:, :, :], ACT.Exp, after=[vec.line.now()])
        seq(V.tensor_reduce, psel[:, :, 0], e4[:, :, :], AX, ALU.add)
        seq(V.reciprocal, psel[:, :, :], psel[:, :, :])
        seq(V.tensor_tensor, prod[:, :, :, :], lg[:, :, 4:20].rearrange("p t (g e) -> p t g e", g=4),
            ohg[:, :, :].unsqueeze(3).broadcast_to([P, TT, 4, 4]), ALU.mult)
        seq(V.tensor_reduce, el[:, :, :], prod[:, :, :, :].rearrange("p t g e -> p t e g"), AX, ALU.add)
        first_max(oh1, el[:, :, :], m1)
        seq(V.scalar_tensor_tensor, el[:, :, :], oh1[:, :, :], NEG, el[:, :, :], ALU.mult, ALU.add)
        first_max(oh2, el[:, :, :], m2)
        seq(V.tensor_tensor, m2[:, :, :], m2[:, :, :], m1[:, :, :], ALU.subtract)
        act.do(S.activation, m2[:, :, :], m2[:, :, :], ACT.Exp, after=[vec.line.now()])
        seq(V.tensor_scalar, m1[:, :, :], m2[:, :, :], 1.0, None, ALU.add)
        seq(V.reciprocal, m1[:, :, :], m1[:, :, :])
        seq(V.tensor_tensor, wts[:, 0, :], m1[:, :, 0], psel[:, :, 0], ALU.mult)
        seq(V.tensor_tensor, wts[:, 1, :], wts[:, 0, :], m2[:, :, 0], ALU.mult)
        for a, oh in zip(A, (oh1, oh2)):
            seq(V.tensor_tensor, a[:, :, :].rearrange("p t (g e) -> p t g e", g=4),
                ohg[:, :, :].unsqueeze(3).broadcast_to([P, TT, 4, 4]),
                oh[:, :, :].unsqueeze(2).broadcast_to([P, TT, 4, 4]), ALU.mult)
        seq(V.tensor_tensor, asum[:, :, :], A[0][:, :, :], A[1][:, :, :], ALU.add)
        pe.need(vec.line.now())
        for t4 in range(TT):
            dst = bank[1][:, t4 * NE:(t4 + 1) * NE]
            for u in range(t4 + 1):
                pe.do(PE.matmul, dst, const("before") if u == t4 else ones[:, :], asum[:, u, :], start=u == 0,
                      stop=u == t4)
        for u in range(TT):
            pe.do(PE.matmul, bank[1][:, TT * NE:(TT + 1) * NE], ones[:, :], asum[:, u, :], start=u == 0, stop=u == TT - 1)
        seq(V.tensor_copy, cnt[:, :], bank[1][:, TT * NE:(TT + 1) * NE])
        seq(V.tensor_scalar, nb[:, :], cnt[:, :], 0.0, None, ALU.is_gt)
        for m in range(1, TT):
            seq(V.scalar_tensor_tensor, nb[:, :], cnt[:, :], float(P * m), nb[:, :], ALU.is_gt, ALU.add)
        seq(V.tensor_tensor_scan, inc[:, :], ones[:, 0:NE], nb[:, :], 0.0, ALU.mult, ALU.add)
        seq(V.tensor_tensor, st_[:, :], inc[:, :], nb[:, :], ALU.subtract)
        seq(V.tensor_scalar, st_[:, :], st_[:, :], float(P), None, ALU.mult)
        seq(V.tensor_tensor, slot[:, :, :], bank[1][:, 0:TT * NE].rearrange("p (t n) -> p t n", t=TT),
            st_[:, :].unsqueeze(1).broadcast_to([P, TT, NE]), ALU.add)
        for j in range(2):
            seq(V.tensor_tensor, A[j][:, :, :], A[j][:, :, :], slot[:, :, :], ALU.mult)
            seq(V.tensor_reduce, g1[:, :, 0], A[j][:, :, :], AX, ALU.add)
            seq(V.tensor_copy, slots_u[:, j, :], g1[:, :, 0])
        seq(V.tensor_tensor, cmpb[:, :, :], inc[:, :].unsqueeze(1).broadcast_to([P, BLOCKS, NE]),
            const("iota")[:, 0:BLOCKS].unsqueeze(2).broadcast_to([P, BLOCKS, NE]), ALU.is_le)
        seq(V.tensor_reduce, etf[:, :], cmpb[:, :, :], AX, ALU.add)
        seq(V.tensor_scalar, etf[:, :], etf[:, :], float(NE - 1), None, ALU.min)
        table = seq(V.tensor_copy, etab_u[:, :], etf[:, :])
        tok_u = sbuf("token_ids", [P, TT], U32, r_ctx)
        seq(V.tensor_copy, tok_u[:, :], const("token"))
        lsc = line("slots_scattered")
        pool.need(vec.line.now(), lz.now())
        for j in range(2):
            for t4 in range(TT):
                G.indirect_dma_start(idxd, bass.IndirectOffsetOnAxis(ap=slots_u[:, j, t4:t4 + 1], axis=0),
                                     tok_u[:, t4:t4 + 1], None).then_inc(lsc.sem, 16)
                lsc.n += 16
        pool.need(lsc.now(), lh2.now())
        vec.need(lh2.now())
        act.need(lh2.now(), lsc.now())
        join()
        r_ctx.close()

        e_ctx = ExitStack()
        raw = [*(r[:, :] for r in ring), *(sbuf(f"ring{i}", [P, HALF], F32, e_ctx)[:, :] for i in range(4, UNITS))]
        high = [wh[:, 0, :], wh[:, 1, :], *(XH[:, 2 * i:2 * i + 2, :].rearrange("p a t -> p (a t)") for i in range(4))]
        low = [wl[:, 0, :], wl[:, 1, :], *(XL[:, 2 * i:2 * i + 2, :].rearrange("p a t -> p (a t)") for i in range(4))]
        idx = sbuf("slot_tokens", [P, BLOCKS], U32, e_ctx)
        idx_now = sbuf("tokens_now", [P, 1], U32, e_ctx)
        hg = sbuf("gathered", [P, D], F32, e_ctx)
        hgh, hgl = sbuf("gathered_high", [P, KC, P], F32R, e_ctx), sbuf("gathered_low", [P, KC, P], F32R, e_ctx)
        sg, av = sbuf("expert_silu", [P, DE], F32, e_ctx), sbuf("expert_hidden", [P, DE], F32, e_ctx)
        ath, atl = sbuf("hidden_high", [P, 4, P], F32R, e_ctx), sbuf("hidden_low", [P, 4, P], F32R, e_ctx)
        yt = sbuf("expert_out", [P, D], F32, e_ctx)
        unit_landed = [line(f"unit_landed{q}") for q in range(UNITS)]
        l_high, l_split, l_used = line("unit_high_done"), line("unit_split_done"), line("unit_used_done")
        l_now, l_seen = line("index_set"), line("index_seen")
        l_idx, l_hg, l_turn, l_hgh, l_hgl = (line(n) for n in (
            "index_landed", "rows_gathered", "rows_turned", "gathered_high_done", "gathered_low_done"))
        l_silu, l_av, l_at, l_ath, l_atl, l_y0, l_y1, l_st = (line(n) for n in (
            "silu_done", "hidden_done", "hidden_turned", "hidden_high_done", "hidden_low_done", "out0_done",
            "out1_done", "out_stored"))
        l_table, table_in = line("table_in"), sbuf("table_probe", [1, 1], F32, e_ctx)
        for q, lines in ((act, (l_silu, l_ath, l_y0, l_hgh, l_high, l_table, l_st)), (vec, (l_av, l_atl, l_y1, l_hgl, l_split)),
                         (pe, (l_at, l_used))):
            for ln in lines:
                q.eng.sem_inc(ln.sem, 16)

        def reach(eng, ln, value):
            eng.wait_ge(ln.sem, value + 16)
        wg = I["w_gate_2"][0].rearrange("e (k p) n -> e p k n", p=P)
        wu = I["w_up_2"][0].rearrange("e (k p) n -> e p k n", p=P)
        wd = I["w_down_2"][0].rearrange("e (k p) n -> e p k n", p=P)

        def gather(b):
            if not isinstance(b, int) or b:
                G.wait_ge(l_turn.sem, b)
            G.tensor_copy(idx_now[:, :], idx[:, bass.ds(b, 1)]).then_inc(l_now.sem, 1)
            G.wait_ge(l_now.sem, b + 1)
            G.sem_inc(l_seen.sem, 1)
            G.indirect_dma_start(hg[:, :], None, h2d, bass.IndirectOffsetOnAxis(ap=idx_now[:, 0:1], axis=0)).then_inc(
                l_hg.sem, 16)

        def turn_rows(b):
            PE.wait_ge(l_hg.sem, b * 16 + 16)
            reach(PE, l_hgl, b * 2)
            for k in range(KC):
                t = PE.transpose(bank[4 + k // 4][:, (k % 4) * P:(k % 4 + 1) * P], hg[:, k * P:(k + 1) * P], ident)
            t.then_inc(l_turn.sem, 1)

        def split_rows(b, half):
            src = bank[4 + half][:, :].rearrange("p (k n) -> p k n", k=4)
            S.wait_ge(l_turn.sem, b + 1)
            S.copy(hgh[:, 4 * half:4 * half + 4, :], src).then_inc(l_hgh.sem, 1)
            reach(V, l_hgh, b * 2 + (half + 1))
            V.tensor_tensor(hgl[:, 4 * half:4 * half + 4, :], src, hgh[:, 4 * half:4 * half + 4, :].bitcast(F32),
                            ALU.subtract).then_inc(l_hgl.sem, 1)

        def fetch(b, e, q, first=False):
            if not first:
                reach(SP, l_split, b * UNITS + (q + 1 - UNITS))
            if q < 8:
                src = (wg if q < 4 else wu)[bass.ds(e, 1), :, 2 * (q % 4):2 * (q % 4) + 2, :].rearrange(
                    "e p k n -> (e p) k n")
                dst = raw[q].rearrange("p (k n) -> p k n", k=2)
            else:
                src = wd[bass.ds(e, 1), :, q - 8, :].rearrange("e p n -> (e p) n")
                dst = raw[q]
            SP.dma_start(dst, src).then_inc(unit_landed[q].sem, 16)

        def split_unit(b, q, first=False):
            g, s = b * UNITS + q, q % HELD
            S.wait_ge(unit_landed[q].sem, b * 16 + 16)
            if not first:
                reach(S, l_used, g - (HELD - 1))
            S.copy(high[s], raw[q]).then_inc(l_high.sem, 1)
            reach(V, l_high, g + 1)
            V.tensor_tensor(low[s], raw[q], high[s].bitcast(F32), ALU.subtract).then_inc(l_split.sem, 1)

        for q in engines:
            q.need(*[x for b in range(8) for x in bank_free[b]])
        with nc.allow_non_contiguous_dma(reason="once, 12 KB"):
            load(pool, l_idx, idx[:, :], idxd.rearrange("(b p) o -> p (b o)", p=P))
        pool.need(l_idx.now())
        gather(0)
        turn_rows(0)
        for half in range(2):
            split_rows(0, half)
        SP.wait_ge(vec.line.sem, table[1])
        e = SP.value_load(etab_u[0:1, 0:1], min_val=0, max_val=NE - 1)
        for q in range(UNITS):
            if q == len(ring):
                sp.need(lh2.now(), lz.now(), lsc.now(), vec.line.now(), act.line.now(), pe.line.now())
            fetch(0, e, q, first=True)
        for q in range(AHEAD):
            split_unit(0, q, first=True)
        def block(b, last=False):
            if not last:
                e = SP.value_load(etab_u[0:1, bass.ds(b + 1, 1)], min_val=0, max_val=NE - 1)
                for q in range(UNITS):
                    fetch(b + 1, e, q)

            def split_ahead(q):
                if q + AHEAD < UNITS:
                    split_unit(b, q + AHEAD)
                elif not last:
                    split_unit(b + 1, q + AHEAD - UNITS)

            def wide(q):
                s = q % HELD
                reach(PE, l_split, b * UNITS + (q + 1))
                for c in range(2):
                    k = 2 * (q % 4) + c
                    w_h, w_l = high[s][:, c * DE:(c + 1) * DE], low[s][:, c * DE:(c + 1) * DE]
                    last = three_pass(bank[q // 4][:, :], hgh[:, k, :], hgl[:, k, :], w_h, w_l, k == 0, k == KC - 1)
                last.then_inc(l_used.sem, 1)

            reach(S, l_table, b)
            S.activation(table_in[:, :], ones[0:1, 0:1], ACT.Silu).then_inc(l_table.sem, 1)
            reach(PE, l_hgl, b * 2 + 2)
            reach(PE, l_silu, b)
            for q in range(4):
                split_ahead(q)
                wide(q)
            reach(S, l_used, b * UNITS + 4)
            reach(S, l_av, b)
            S.activation(sg[:, :], bank[0][:, :], ACT.Silu).then_inc(l_silu.sem, 1)
            reach(PE, l_av, b)
            for q in range(4, 8):
                if q < 7:
                    split_ahead(q)
                wide(q)
            reach(V, l_used, b * UNITS + 8)
            reach(V, l_silu, b + 1)
            reach(V, l_at, b)
            V.tensor_tensor(av[:, :], sg[:, :], bank[1][:, :], ALU.mult).then_inc(l_av.sem, 1)
            reach(PE, l_av, b + 1)
            reach(PE, l_atl, b)
            for k in range(4):
                t = PE.transpose(bank[6][:, k * P:(k + 1) * P], av[:, k * P:(k + 1) * P], ident)
            t.then_inc(l_at.sem, 1)
            src6 = bank[6][:, :].rearrange("p (k n) -> p k n", k=4)
            reach(S, l_at, b + 1)
            reach(S, l_used, b * UNITS)
            S.copy(ath[:, :, :], src6).then_inc(l_ath.sem, 1)
            reach(V, l_ath, b + 1)
            V.tensor_tensor(atl[:, :, :], src6, ath[:, :, :].bitcast(F32), ALU.subtract).then_inc(l_atl.sem, 1)
            split_ahead(7)
            if not last:
                gather(b + 1)
                turn_rows(b + 1)
            reach(PE, l_atl, b + 1)
            reach(PE, l_y0, b)
            reach(PE, l_y1, b)
            for q in range(8, UNITS):
                split_ahead(q)
                if q < 10 and not last:
                    split_rows(b + 1, q - 8)
                s, k = q % HELD, q - 8
                reach(PE, l_split, b * UNITS + (q + 1))
                for n in range(2):
                    t = three_pass(bank[2 + n][:, :], ath[:, k, :], atl[:, k, :], high[s][:, n * 512:(n + 1) * 512],
                                   low[s][:, n * 512:(n + 1) * 512], k == 0, k == 3)
                t.then_inc(l_used.sem, 1)
            reach(S, l_used, b * UNITS + UNITS)
            reach(S, l_st, b * 16)
            S.copy(yt[:, 0:512], bank[2][:, :]).then_inc(l_y0.sem, 1)
            reach(V, l_used, b * UNITS + UNITS)
            reach(V, l_st, b * 16)
            V.tensor_copy(yt[:, 512:1024], bank[3][:, :]).then_inc(l_y1.sem, 1)
            reach(SP, l_y0, b + 1)
            reach(SP, l_y1, b + 1)
            SP.dma_start(yd[bass.ds(b * P, P), :], yt[:, :]).then_inc(l_st.sem, 16)

        with nc.Fori(0, BLOCKS - 1, 1, engines=[x.eng.engine for x in (vec, act, pe, sp, pool)]) as b:
            block(b)
        block(BLOCKS - 1, last=True)
        l_split.n = UNITS * BLOCKS + 16
        l_st.n, l_hgl.n = 16 * BLOCKS + 16, 2 * BLOCKS + 16
        for q in engines:
            q.need(l_st.now(), l_hgl.now(), l_split.now())
        join()
        e_ctx.close()

        ga, gb = sbuf("out_first", [P, 2, D]), sbuf("out_second", [P, 2, D])
        fo, grow = sbuf("final", [P, 2, D]), sbuf("gain_row", [P, D])
        ss = sbuf("sum_squares", [P, TT])
        lga, lout = line("pairs_gathered"), [line(f"output_stored{z}") for z in range(2)]
        for k in range(KC):
            t = pe.do(PE.matmul, bank[6 + k // 4][:, (k % 4) * P:(k % 4 + 1) * P], POST_FFN[:, k:k + 1].broadcast_to([P, P]),
                      ident, start=True, stop=True)
        for half in range(2):
            gain_ready = vec.do(V.tensor_copy, grow[:, half * 512:(half + 1) * 512], bank[6 + half][:, :], after=[t])
        ends = [[], []]
        for t4 in range(TT):
            z = t4 % 2
            pool.need(*ends[z])
            for j, dst in enumerate((ga, gb)):
                G.indirect_dma_start(dst[:, z, :], None, yd,
                                     bass.IndirectOffsetOnAxis(ap=slots_u[:, j, t4:t4 + 1], axis=0)).then_inc(lga.sem, 16)
                lga.n += 16
            pool.need(lga.now())
            b = 2 * z
            pe.need(*bank_free[b], *bank_free[b + 1])
            for k in range(KC):
                tx = pe.do(PE.transpose, bank[b + k // 4][:, (k % 4) * P:(k % 4 + 1) * P], X[:, k, t4 * P:(t4 + 1) * P],
                           ident)
            t = vec.do(V.tensor_scalar, ga[:, z, :], ga[:, z, :], wts[:, 0, t4:t4 + 1], None, ALU.mult, after=[lga.now()])
            t = vec.do(V.scalar_tensor_tensor, ga[:, z, :], gb[:, z, :], wts[:, 1, t4:t4 + 1], ga[:, z, :], ALU.mult,
                       ALU.add, after=[t])
            t = act.do(S.activation, gb[:, z, :], ga[:, z, :], ACT.Square, accum_out=ss[:, t4:t4 + 1], after=[t])
            t = vec.do(V.tensor_scalar, ss[:, t4:t4 + 1], ss[:, t4:t4 + 1], 1.0 / D, EPS, ALU.mult, ALU.add, after=[t])
            t = vec.do(V.reciprocal, ss[:, t4:t4 + 1], ss[:, t4:t4 + 1], after=[t])
            t = act.do(S.activation, ss[:, t4:t4 + 1], ss[:, t4:t4 + 1], ACT.Sqrt, after=[t])
            t = vec.do(V.scalar_tensor_tensor, fo[:, z, :], ga[:, z, :], ss[:, t4:t4 + 1], grow[:, :], ALU.mult,
                       ALU.mult, after=[t, gain_ready, *ends[z]])
            for half in range(2):
                cols = slice(half * 512, (half + 1) * 512)
                tt_ = vec.do(V.tensor_tensor, fo[:, z, cols], fo[:, z, cols], bank[b + half][:, :], ALU.add, after=[t, tx])
                bank_free[b + half] = [tt_]
            ends[z] = [tt_, load(act, lout[z], out[0, t4 * P:(t4 + 1) * P, :], fo[:, z, :], after=[tt_])]
        for q in (act, sp):
            q.need(lout[0].now(), lout[1].now())


INPUTS = [
    "x", "mem", "norm_mix_pre", "norm_mix_post", "norm_ffn_pre", "norm_ffn_post", "mem_norm", "w_mem_kv",
    "w_in_a", "conv_w", "conv_b", "w_gate_r", "b_gate_r", "w_gate_i", "b_gate_i", "lru_lambda", "norm_kv",
    "w_kv_shared", "w_in_b", "sinks", "w_out", "w_ffn_in", "w_ffn_out", "c_2", "ctx_2", "c_ctx_2", "w_ada_2",
    "b_ada_2", "g_pre_mix_2", "g_post_mix_2", "g_pre_ffn_2", "g_post_ffn_2", "w_in_2", "conv_w_2", "conv_b_2",
    "w_q_2", "w_k_2", "w_v_2", "w_if_fwd_2", "b_if_fwd_2", "w_if_bwd_2", "b_if_bwd_2", "mlstm_norm_w_2",
    "mlstm_skip_2", "w_fourier_2", "w_out_2", "w_router_group_2", "b_router_group_2", "w_router_expert_2",
    "b_router_expert_2", "w_gate_2", "w_up_2", "w_down_2",
]


def kernel(**inputs):
    import concourse.bacc as bacc
    from concourse.bass_utils import run_bass_kernel_spmd

    nc = bacc.Bacc("TRN2", target_bir_lowering=False, num_devices=1)
    constants, _, dft_t = shape_constants()
    given = {name: np.ascontiguousarray(inputs[name]) for name in INPUTS}
    given["constants"], given["dft_t"] = constants, dft_t
    arrays, aps = {}, {}
    for name, a in given.items():
        arrays[f"in_{name}"] = a
        aps[name] = nc.dram_tensor(f"in_{name}", a.shape, mybir.dt.from_np(a.dtype), kind="ExternalInput").ap()
    out = nc.dram_tensor("out_hidden", (1, T, D), F32, kind="ExternalOutput").ap()
    program(nc, aps, out)
    r = run_bass_kernel_spmd(nc, [arrays], core_ids=[0])
    return r.results[0]["out_hidden"]
```
